# Optimizing a Trainium2 kernel written in Bass

```python
import math
import jax, jax.numpy as jnp
from jax import lax
import numpy as np

D_MODEL = 1024
BATCH = 1
SEQ = 2048
DEPTH = 1

D_S5 = 256
S5_GROUP = 16
S5_GROUPS = D_S5 // S5_GROUP
S5_STATE = 64
D_RG = 256
RG_BLOCKS = 8
RG_BLOCK = D_RG // RG_BLOCKS
RG_CONV = 4
RG_C = 8.0
N_HEADS = 8
N_KV_HEADS = 2
HEAD_DIM = 64
D_ATTN = N_HEADS * HEAD_DIM
KV_DIM = N_KV_HEADS * HEAD_DIM
Q_PER_KV = N_HEADS // N_KV_HEADS
IDX_HEADS = 8
IDX_DIM = 64
TOPK_MAX = 256
Q_BLOCK = 128
D_MIX = D_S5 + D_RG + D_ATTN
ROPE_THETA = 10000.0
D_FF = -(-8 * D_MODEL // (3 * 256)) * 256
D_PLE = 256
ALPHA = (2.0 * DEPTH) ** 0.25
BETA = (8.0 * DEPTH) ** -0.25
LN_EPS = 1e-5
IN_SIZES = (D_S5, D_RG, D_RG, D_ATTN, KV_DIM, KV_DIM, IDX_HEADS * IDX_DIM, IDX_DIM, IDX_HEADS)
N_IN = sum(IN_SIZES)

kernel_name = "hybrid_s5_rglru_dsa_deepnorm"

def _split_points():
    pts, acc = [], 0
    for s in IN_SIZES[:-1]:
        acc += s
        pts.append(acc)
    return pts

def layer_norm(x, g, b):
    xf = x.astype(jnp.float32)
    mu = jnp.mean(xf, axis=-1, keepdims=True)
    var = jnp.mean(jnp.square(xf - mu), axis=-1, keepdims=True)
    return ((xf - mu) * lax.rsqrt(var + LN_EPS) * g + b).astype(x.dtype)

def rope_tables(positions, dim):
    inv = ROPE_THETA ** (-jnp.arange(0, dim, 2, dtype=jnp.float32) / dim)
    ang = positions.astype(jnp.float32)[..., None] * inv
    return jnp.cos(ang)[:, :, None, :], jnp.sin(ang)[:, :, None, :]

def rope(x, cos, sin):
    cos = cos.astype(x.dtype)
    sin = sin.astype(x.dtype)
    x1, x2 = jnp.split(x, 2, axis=-1)
    return jnp.concatenate([x1 * cos - x2 * sin, x2 * cos + x1 * sin], axis=-1)

def _complex_linear_combine(e1, e2):
    a1r, a1i, b1r, b1i = e1
    a2r, a2i, b2r, b2i = e2
    ar = a2r * a1r - a2i * a1i
    ai = a2r * a1i + a2i * a1r
    br = a2r * b1r - a2i * b1i + b2r
    bi = a2r * b1i + a2i * b1r + b2i
    return ar, ai, br, bi

def _real_linear_combine(e1, e2):
    a1, b1 = e1
    a2, b2 = e2
    return a2 * a1, a2 * b1 + b2

def s5_mixer(u, lam_re, lam_im, log_step, b_re, b_im, c_re, c_im, d_skip, w_glu, b_glu):
    bsz, L, _ = u.shape
    uf = u.astype(jnp.float32)
    ug = uf.reshape(bsz, L, S5_GROUPS, S5_GROUP)
    lr = lam_re.astype(jnp.float32)
    li = lam_im.astype(jnp.float32)
    step = jnp.exp(log_step.astype(jnp.float32))[:, None]
    mag = jnp.exp(lr * step)
    ar = mag * jnp.cos(li * step)
    ai = mag * jnp.sin(li * step)
    den = lr * lr + li * li
    nr, ni = ar - 1.0, ai
    cr = (nr * lr + ni * li) / den
    ci = (ni * lr - nr * li) / den
    br = b_re.astype(jnp.float32)
    bi = b_im.astype(jnp.float32)
    bbr = cr[..., None] * br - ci[..., None] * bi
    bbi = cr[..., None] * bi + ci[..., None] * br
    bu_r = jnp.einsum('blgc,gpc->blgp', ug, bbr)
    bu_i = jnp.einsum('blgc,gpc->blgp', ug, bbi)
    a_r = jnp.broadcast_to(ar, bu_r.shape)
    a_i = jnp.broadcast_to(ai, bu_r.shape)
    _, _, xr, xi = lax.associative_scan(_complex_linear_combine, (a_r, a_i, bu_r, bu_i), axis=1)
    y = (jnp.einsum('blgp,gcp->blgc', xr, c_re.astype(jnp.float32))
         - jnp.einsum('blgp,gcp->blgc', xi, c_im.astype(jnp.float32)))
    y = y.reshape(bsz, L, D_S5) + d_skip.astype(jnp.float32) * uf
    y = jax.nn.gelu(y)
    y = y * jax.nn.sigmoid(y @ w_glu.astype(jnp.float32) + b_glu.astype(jnp.float32))
    return y.astype(u.dtype)

def rglru_mixer(xr, gate, conv_w, conv_b, wa, ba, wx, bx, lam):
    bsz, L, _ = xr.shape
    xpad = jnp.pad(xr, ((0, 0), (RG_CONV - 1, 0), (0, 0)))
    xc = conv_b
    for k in range(RG_CONV):
        xc = xc + conv_w[k] * xpad[:, k:k + L]
    xb = xc.reshape(bsz, L, RG_BLOCKS, RG_BLOCK)
    r = jax.nn.sigmoid(jnp.einsum('blhi,hij->blhj', xb, wa).reshape(bsz, L, D_RG) + ba)
    ig = jax.nn.sigmoid(jnp.einsum('blhi,hij->blhj', xb, wx).reshape(bsz, L, D_RG) + bx)
    log_a = -RG_C * r.astype(jnp.float32) * jax.nn.softplus(-lam.astype(jnp.float32))
    a = jnp.exp(log_a)
    mult = jnp.sqrt(-jnp.expm1(2.0 * log_a))
    bvals = mult * (ig * xc).astype(jnp.float32)
    _, h = lax.associative_scan(_real_linear_combine, (a, bvals), axis=1)
    return h.astype(xr.dtype) * jax.nn.gelu(gate)

def dsa_mixer(q, k, v, qi, ki, wi, positions):
    bsz, L, _ = q.shape
    q = q.reshape(bsz, L, N_HEADS, HEAD_DIM)
    k = k.reshape(bsz, L, N_KV_HEADS, HEAD_DIM)
    v = v.reshape(bsz, L, N_KV_HEADS, HEAD_DIM)
    qi = qi.reshape(bsz, L, IDX_HEADS, IDX_DIM)
    cos, sin = rope_tables(positions, HEAD_DIM)
    q = rope(q, cos, sin)
    k = rope(k, cos, sin)
    qi = rope(qi, cos, sin)
    ki = rope(ki[:, :, None, :], cos, sin)[:, :, 0]
    top = min(TOPK_MAX, L // 4)
    nblk = L // Q_BLOCK
    q_b = q.reshape(bsz, nblk, Q_BLOCK, N_KV_HEADS, Q_PER_KV, HEAD_DIM).transpose(1, 0, 2, 3, 4, 5)
    qi_b = qi.reshape(bsz, nblk, Q_BLOCK, IDX_HEADS, IDX_DIM).transpose(1, 0, 2, 3, 4)
    wi_b = wi.reshape(bsz, nblk, Q_BLOCK, IDX_HEADS).transpose(1, 0, 2, 3)
    key_pos = jnp.arange(L)
    idx_scale = (IDX_HEADS * IDX_DIM) ** -0.5
    att_scale = HEAD_DIM ** -0.5

    def block(args):
        blk, qb, qib, wib = args
        t = blk * Q_BLOCK + jnp.arange(Q_BLOCK)
        causal = key_pos[None, :] <= t[:, None]
        rel = jax.nn.relu(jnp.einsum('bthd,bsd->bths', qib, ki).astype(jnp.float32))
        score = jnp.einsum('bths,bth->bts', rel, wib.astype(jnp.float32)) * idx_scale
        score = jnp.where(causal[None], score, -jnp.inf)
        _, idx = lax.top_k(score, top)
        valid = idx <= t[None, :, None]
        k_sel = jax.vmap(lambda kk, ii: kk[ii])(k, idx)
        v_sel = jax.vmap(lambda vv, ii: vv[ii])(v, idx)
        logits = jnp.einsum('btgrd,btkgd->btgrk', qb, k_sel).astype(jnp.float32) * att_scale
        logits = jnp.where(valid[:, :, None, None, :], logits, -jnp.inf)
        probs = jax.nn.softmax(logits, axis=-1).astype(v.dtype)
        o = jnp.einsum('btgrk,btkgd->btgrd', probs, v_sel)
        return o.reshape(bsz, Q_BLOCK, D_ATTN)

    out = lax.map(block, (jnp.arange(nblk), q_b, qi_b, wi_b))
    return out.transpose(1, 0, 2, 3).reshape(bsz, L, D_ATTN)

def setup_inputs(seed: int = 0) -> dict:
    key = jax.random.key(seed)
    ks = iter(jax.random.split(key, 48))
    f32 = jnp.float32

    def nrm(shape, scale):
        return scale * jax.random.normal(next(ks), shape, f32)

    x = nrm((BATCH, SEQ, D_MODEL), 1.0)
    p = nrm((DEPTH, BATCH, SEQ, D_PLE), 1.0)
    offs = jax.random.randint(next(ks), (BATCH, 1), 0, 4096, dtype=jnp.int32)
    positions = (offs + jnp.arange(SEQ, dtype=jnp.int32)[None, :]).astype(jnp.int32)
    ln_emb_g = 1.0 + nrm((D_MODEL,), 0.02)
    ln_emb_b = nrm((D_MODEL,), 0.02)
    w_in = nrm((DEPTH, D_MODEL, N_IN), D_MODEL ** -0.5)
    s5_lam_re = -0.5 + nrm((DEPTH, S5_GROUPS, S5_STATE), 0.01)
    s5_lam_im = math.pi * jnp.arange(S5_STATE, dtype=f32) + nrm((DEPTH, S5_GROUPS, S5_STATE), 0.01)
    s5_log_step = jax.random.uniform(next(ks), (DEPTH, S5_GROUPS), f32, math.log(1e-3), math.log(1e-1))
    s5_b_re = nrm((DEPTH, S5_GROUPS, S5_STATE, S5_GROUP), (2 * S5_GROUP) ** -0.5)
    s5_b_im = nrm((DEPTH, S5_GROUPS, S5_STATE, S5_GROUP), (2 * S5_GROUP) ** -0.5)
    s5_c_re = nrm((DEPTH, S5_GROUPS, S5_GROUP, S5_STATE), S5_STATE ** -0.5)
    s5_c_im = nrm((DEPTH, S5_GROUPS, S5_GROUP, S5_STATE), S5_STATE ** -0.5)
    s5_d = nrm((DEPTH, D_S5), 1.0)
    s5_w_glu = nrm((DEPTH, D_S5, D_S5), D_S5 ** -0.5)
    s5_b_glu = nrm((DEPTH, D_S5), 0.02)
    rg_conv_w = nrm((DEPTH, RG_CONV, D_RG), RG_CONV ** -0.5)
    rg_conv_b = nrm((DEPTH, D_RG), 0.02)
    rg_wa = nrm((DEPTH, RG_BLOCKS, RG_BLOCK, RG_BLOCK), RG_BLOCK ** -0.5)
    rg_ba = nrm((DEPTH, D_RG), 0.02)
    rg_wx = nrm((DEPTH, RG_BLOCKS, RG_BLOCK, RG_BLOCK), RG_BLOCK ** -0.5)
    rg_bx = nrm((DEPTH, D_RG), 0.02)
    a_c = jax.random.uniform(next(ks), (DEPTH, D_RG), f32, 0.9, 0.999)
    a0 = a_c ** (1.0 / RG_C)
    rg_lam = jnp.log(a0) - jnp.log1p(-a0)
    w_out = nrm((DEPTH, D_MIX, D_MODEL), BETA * D_MIX ** -0.5)
    ln1_g = 1.0 + nrm((DEPTH, D_MODEL), 0.02)
    ln1_b = nrm((DEPTH, D_MODEL), 0.02)
    ffn_w_up = nrm((DEPTH, D_MODEL, 2 * D_FF), D_MODEL ** -0.5)
    ffn_w_down = nrm((DEPTH, D_FF, D_MODEL), BETA * D_FF ** -0.5)
    ple_w_gate = nrm((DEPTH, D_MODEL, D_MODEL), D_MODEL ** -0.5)
    ple_w_proj = nrm((DEPTH, D_PLE, D_MODEL), BETA * D_PLE ** -0.5)
    ln2_g = 1.0 + nrm((DEPTH, D_MODEL), 0.02)
    ln2_b = nrm((DEPTH, D_MODEL), 0.02)
    return {
        "x": x, "p": p, "positions": positions,
        "ln_emb_g": ln_emb_g, "ln_emb_b": ln_emb_b, "w_in": w_in,
        "s5_lam_re": s5_lam_re, "s5_lam_im": s5_lam_im, "s5_log_step": s5_log_step,
        "s5_b_re": s5_b_re, "s5_b_im": s5_b_im, "s5_c_re": s5_c_re, "s5_c_im": s5_c_im,
        "s5_d": s5_d, "s5_w_glu": s5_w_glu, "s5_b_glu": s5_b_glu,
        "rg_conv_w": rg_conv_w, "rg_conv_b": rg_conv_b, "rg_wa": rg_wa, "rg_ba": rg_ba,
        "rg_wx": rg_wx, "rg_bx": rg_bx, "rg_lam": rg_lam,
        "w_out": w_out, "ln1_g": ln1_g, "ln1_b": ln1_b,
        "ffn_w_up": ffn_w_up, "ffn_w_down": ffn_w_down,
        "ple_w_gate": ple_w_gate, "ple_w_proj": ple_w_proj,
        "ln2_g": ln2_g, "ln2_b": ln2_b,
    }

def reference(x, p, positions, ln_emb_g, ln_emb_b, w_in,
              s5_lam_re, s5_lam_im, s5_log_step, s5_b_re, s5_b_im, s5_c_re, s5_c_im,
              s5_d, s5_w_glu, s5_b_glu,
              rg_conv_w, rg_conv_b, rg_wa, rg_ba, rg_wx, rg_bx, rg_lam,
              w_out, ln1_g, ln1_b, ffn_w_up, ffn_w_down, ple_w_gate, ple_w_proj,
              ln2_g, ln2_b):
    pts = _split_points()
    h = layer_norm(x, ln_emb_g, ln_emb_b)
    for i in range(DEPTH):
        proj = h @ w_in[i]
        u_s5, x_rg, g_rg, q, k, v, qi, ki, wi = jnp.split(proj, pts, axis=-1)
        y_s5 = s5_mixer(u_s5, s5_lam_re[i], s5_lam_im[i], s5_log_step[i], s5_b_re[i], s5_b_im[i],
                        s5_c_re[i], s5_c_im[i], s5_d[i], s5_w_glu[i], s5_b_glu[i])
        y_rg = rglru_mixer(x_rg, g_rg, rg_conv_w[i], rg_conv_b[i], rg_wa[i], rg_ba[i],
                           rg_wx[i], rg_bx[i], rg_lam[i])
        y_at = dsa_mixer(q, k, v, qi, ki, wi, positions)
        mix = jnp.concatenate([y_s5, y_rg, y_at], axis=-1) @ w_out[i]
        h = layer_norm(ALPHA * h + mix, ln1_g[i], ln1_b[i])
        gate_up = h @ ffn_w_up[i]
        g_ff, u_ff = jnp.split(gate_up, 2, axis=-1)
        ffn = (jax.nn.silu(g_ff) * u_ff) @ ffn_w_down[i]
        ple = jax.nn.sigmoid(h @ ple_w_gate[i]) * (p[i] @ ple_w_proj[i])
        h = layer_norm(ALPHA * h + ffn + ple, ln2_g[i], ln2_b[i])
    return h


_drawn_inputs = setup_inputs


def setup_inputs(seed=0):
    import zlib

    import numpy as np

    out = dict(_drawn_inputs(seed))
    spreads = {}
    factors = {'ln_emb_g': 2.824,
     's5_lam_re': 64.0,
     's5_lam_im': 64.0,
     's5_log_step': 64.0,
     's5_b_re': 64.0,
     's5_b_im': 64.0,
     's5_c_re': 64.0,
     's5_c_im': 64.0,
     's5_b_glu': 64.0,
     'rg_conv_b': 3.605,
     'rg_ba': 28.691,
     'rg_bx': 29.082,
     'ln1_g': 2.817,
     'ln1_b': 2.762,
     'ln2_g': 7.652,
     'ln2_b': 8.021}
    for name, (base, spread) in spreads.items():
        noise = np.random.default_rng([zlib.crc32(name.encode()), seed]).standard_normal(out[name].shape)
        drawn = base * np.exp(spread * noise) if base else spread * noise
        out[name] = __import__('jax').numpy.asarray(drawn.astype(out[name].dtype))
    for name, factor in factors.items():
        out[name] = (out[name] * factor).astype(out[name].dtype)
    return out
```

```python
import math
from contextlib import ExitStack

import numpy as np
import concourse.bass as bass
from concourse import mybir

P = 128
D = 1024
SEQ = 2048
SB = 512
NSB = SEQ // SB
R = SB // P
KT = D // P
D_S5, S5_GROUP, S5_GROUPS, S5_STATE = 256, 16, 16, 64
NST = S5_GROUPS * S5_STATE // P
TW = 256
SUBS = SB // TW
STEPS = SUBS * NST
RG_CONV = 4
HEADS, HD, KVH = 8, 64, 2
TOPK = 256
N_IN = 2120
D_FF = 2816
NF = D_FF // P
HALF_F = NF // 2
D_PLE = 256
ALPHA = 2.0 ** 0.25
EPS = 1e-5
C_XRG, C_GRG, C_Q, C_K, C_QI, C_KI = 256, 512, 768, 1280, 1536, 2048
UNIT = 512
SLOTS = 4
CH = 2048
MARK = -3.4e38
NEG = -3.0e38
BIG = 1.0e30
TWO_PI = 2 * math.pi
MAGIC = 12582912.0
GELU_C, GELU_K = 0.044715, math.sqrt(2 / math.pi)


def split_two_pi():
    a = np.float32(6.28125)
    b = np.float32(np.floor((TWO_PI - float(a)) * 2 ** 20) / 2 ** 20)
    return float(a), float(b), float(np.float32(TWO_PI - float(a) - float(b)))


def row_tile(s, r):
    return s * R + r


def width(g):
    return (g + 1) * P


def score_at(s, r):
    return sum(width(row_tile(s, i)) for i in range(r))


def pieces(w):
    return [(a, min(UNIT, w - a)) for a in range(0, w, UNIT)]


def selects(g):
    return (g + 1) * P > TOPK


SETUP_ANGLES = 22
SETUP_MATRICES = SETUP_ANGLES + 47
SETUP_PHASES = SETUP_MATRICES + 2 + 6 * 8


MIX_T = KT + 3 * R


def attend_t(s):
    return sum(HEADS * len(pieces(width(row_tile(s, r)))) + 1 for r in range(R)) + KT


def t_start():
    t, at = 2, {}
    at["mix", 0] = t
    t += MIX_T
    at["att", 0] = t
    t += attend_t(0)
    for s in range(NSB):
        if s + 1 < NSB:
            at["mix", s + 1] = t
            t += MIX_T
        at["ffn", s] = t
        t += D_PLE // P
        if s + 1 < NSB:
            at["att", s + 1] = t
            t += attend_t(s + 1)
    return at


T_AT = t_start()


def norm_calls():
    order = [("emb", 0), ("one", 0)]
    for s in range(NSB):
        if s + 1 < NSB:
            order.append(("emb", s + 1))
        order.append(("two", s))
        if s + 1 < NSB:
            order.append(("one", s + 1))
    return {call: n for n, call in enumerate(order)}


NORM = norm_calls()


def idx_jobs(s):
    return [(r, h, a, w) for r in range(R) if selects(row_tile(s, r))
            for h in range(HEADS) for a, w in pieces(width(row_tile(s, r)))]


def before(count, s):
    return sum(count(i) for i in range(s))


def idx_before(s):
    return before(lambda i: len(idx_jobs(i)), s)


def logit_jobs_of(g):
    return HEADS * len(pieces(width(g)))


def logits_before(g):
    return before(logit_jobs_of, g)


def t_attn(g, h):
    s, r = divmod(g, R)
    t = T_AT["att", s]
    for i in range(r):
        t += HEADS * len(pieces(width(row_tile(s, i)))) + 1
    n = len(pieces(width(g)))
    late = r > 0
    return t - late + h * n + (late and h >= 1)


def t_out(g):
    s, r = divmod(g, R)
    if r + 1 < R:
        return t_attn(g + 1, 0) + len(pieces(width(g + 1)))
    return T_AT["att", s] + attend_t(s) - KT - 1


SLOT_LIST = ([("q", 0, r) for r in range(R)] + [("q", 1, r) for r in range(R)]
             + [("kv", None, r) for r in range(R)]
             + [("qi", 0, r) for r in range(R)] + [("qi", 1, r) for r in range(R)]
             + [("end", None, r) for r in range(R)])
GROUP_OF = {"q": 0, "kv": 1, "qi": 2}


def rope_job(slot):
    kind, half, r = slot
    if kind == "kv" or half == 1:
        return GROUP_OF[kind] * R + r
    return None


def transposed_in(slot):
    kind, half, r = slot
    if kind == "kv":
        return r
    if kind == "qi" and half == 0:
        return R + r
    if kind == "end":
        return 2 * R + r
    return None


def chunk_list():
    def mix(s):
        return ([("in_cols", c) for c in (C_XRG, 0, C_GRG)]
                + [("in_rows", C_Q, k) for k in (0, 4)]
                + [("in_cols", C_K)]
                + [("in_rows", C_QI, k) for k in (0, 4)])

    def att(s):
        return [x for c in (0, 1) for x in (("out", c, 0), ("out", c, 4), ("hT", s, c))]

    def ffn(s):
        got = [x for c in (0, 1) for x in (("ple_p", c), ("ple_g", c, 0), ("ple_g", c, 4))]
        for half in (0, 1):
            f0 = half * HALF_F
            got += [("up", f0 + i) for i in range(HALF_F)]
            got += [("down", f0 + a, min(4, HALF_F - a), c) for c in (0, 1) for a in range(0, HALF_F, 4)]
        return got

    order, start = [], {}

    def put(kind, s, part):
        start[kind, s] = len(order)
        order.extend(part)

    put("mix", 0, mix(0))
    put("att", 0, att(0))
    for s in range(NSB):
        if s + 1 < NSB:
            put("mix", s + 1, mix(s + 1))
        put("ffn", s, ffn(s))
        if s + 1 < NSB:
            put("att", s + 1, att(s + 1))
    return order, start


CHUNKS, CHUNK_AT = chunk_list()
DOWN_JOBS = 2 * 2 * R


def trunk_kernel(nc, x, p, positions, ln_emb_g, ln_emb_b, w_in,
                 s5_lam_re, s5_lam_im, s5_log_step, s5_b_re, s5_b_im, s5_c_re, s5_c_im,
                 s5_d, s5_w_glu, s5_b_glu,
                 rg_conv_w, rg_conv_b, rg_wa, rg_ba, rg_wx, rg_bx, rg_lam,
                 w_out, ln1_g, ln1_b, ffn_w_up, ffn_w_down, ple_w_gate, ple_w_proj,
                 ln2_g, ln2_b, out, h_spill, debug=None):
    f32 = mybir.dt.float32
    i32 = mybir.dt.int32
    ALU = mybir.AluOpType
    ACT = mybir.ActivationFunctionType
    X_AXIS = mybir.AxisListType.X

    with ExitStack() as ctx:
        def sb(name, shape, dt=f32):
            return ctx.enter_context(nc.sbuf_tensor(name, shape, dt))

        def sem(name):
            return ctx.enter_context(nc.semaphore(name))

        ring = sb("ring", [P, SLOTS, CH])
        arena = sb("arena", [P, 19, UNIT])
        rows = sb("rows", [P, R, D])
        scores = sb("scores", [P, 58 * P])
        qT = sb("qT", [P, 4, SB])
        mixT = sb("mixT", [P, KT, SB])
        keysT = sb("keysT", [P, 2, SEQ])
        vals = sb("vals", [P, SEQ // P, P])
        phase = sb("phase", [P, NST, 2, TW])
        work = sb("work", [P, 7, UNIT])
        g2 = sb("g2", [P, D])
        b2 = sb("b2", [P, D])
        ident = sb("ident", [P, P])
        alpha_i = sb("alpha_i", [P, P])
        bT = sb("bT", [P, 2, 2, P])
        cT = sb("cT", [P, 2, NST, 32])
        w_glu = sb("w_glu", [P, 2, D_S5])
        w_gates = sb("w_gates", [P, 2, 2, P])
        w_tail = sb("w_tail", [P, KT, N_IN - C_KI])
        cos_t = sb("cos_t", [P, SEQ // P, 32])
        sin_t = sb("sin_t", [P, SEQ // P, 2, 32])
        ln_gb = sb("ln_gb", [P, 4, KT])
        s5c = sb("s5c", [P, 24, NST])
        s5_carry = sb("s5_carry", [P, NST, 2])
        d_col = sb("d_col", [P, 2])
        bglu_col = sb("bglu_col", [P, 2])
        conv_w = sb("conv_w", [P, 2, RG_CONV])
        rgc = sb("rgc", [P, 12, 2])
        halo = sb("halo", [P, 2, RG_CONV - 1])
        rg_carry = sb("rg_carry", [P, 2])
        pos_i = sb("pos_i", [P, SEQ // P], i32)
        pos_f = sb("pos_f", [P, SEQ // P])
        inv_f = sb("inv_f", [P, 32])
        stats = sb("stats", [P, R, 2, 6])
        mv = sb("mv", [P, R, 2])
        var_eps = sb("var_eps", [P, R])
        rstd = sb("rstd", [P, R])
        neg_half = sb("neg_half", [P, R])
        w_idx = sb("w_idx", [P, R, HEADS])
        top8 = sb("top8", [P, 2, 8])
        part_max = sb("part_max", [P, 2, 4])
        neg_max = sb("neg_max", [P, 2])
        row_sum = sb("row_sum", [P, 2, HEADS])
        inv_sum = sb("inv_sum", [P, 2, HEADS])

        act = arena[:, 0:HALF_F, :]
        h1T = arena[:, HALF_F:HALF_F + KT, :]
        hT = arena[:, 0:KT, :]
        relu_buf = arena[:, KT:KT + 3, :]
        prob = [arena[:, 4 * i:4 * i + 4, :].rearrange("p a b -> p (a b)") for i in (0, 1)]
        probT = [arena[:, 8 + 4 * i:12 + 4 * i, :].rearrange("p a b -> p (a b)") for i in (0, 1)]
        qiT = mixT[:, 4:8, :]
        u_t = scores[:, 0:1024].rearrange("p (a b) -> p a b", a=2)
        xr_t = scores[:, 1024:1024 + 2 * 515].rearrange("p (a b) -> p a b", a=2)
        o_ = 1024 + 2 * 515
        gate_t, gelu_t, conv_t, ra_t, ib_t = (
            scores[:, o_ + 1024 * i:o_ + 1024 * (i + 1)].rearrange("p (a b) -> p a b", a=2) for i in range(5))
        a_t = xr_t[:, :, 3:515]
        rope_a, rope_b = rows[:, 0, 0:512], rows[:, 0, 512:1024]
        roped = [rows[:, 1, 0:512], rows[:, 1, 512:1024], rows[:, 2, 0:512], rows[:, 2, 512:1024]]
        s5_m = rows[:, 3, :].rearrange("p (m c t) -> p m c t", m=2, c=2)
        s5_w = [work[:, i, :].rearrange("p (c t) -> p c t", c=2) for i in (0, 1)]
        s5_z = work[:, 2, :].rearrange("p (c t) -> p c t", c=2)
        s5_n = work[:, 3:5, :].rearrange("p m (c t) -> p m c t", c=2)
        s5_x = [work[:, 5 + i, :].rearrange("p (c t) -> p c t", c=2) for i in (0, 1)]
        p_rows = work[:, 0:2, :].rearrange("p a (b c) -> p (a b) c", b=2)
        pT = work[:, 4:6, :]
        half_pp = [mixT[:, 4 + r, :] for r in range(R)]
        tanh_b = [mixT[:, 4, :], mixT[:, 5, :]]
        gate_b = [mixT[:, 6, :], mixT[:, 7, :]]
        up_b = [work[:, 0, :], work[:, 1, :]]
        evac_b = [work[:, 2, :], work[:, 3, :]]
        o_rows = [work[:, 0, :], work[:, 1, :]]
        blk_b = [scores[:, 1024 * i:1024 * i + 256] for i in range(4)]
        blk_c = [scores[:, 4096 + 256 * i:4096 + 256 * (i + 1)] for i in range(2)]
        tmp_a, tmp_b, tmp_c, tmp_d = (mixT[:, i, :] for i in range(4))
        ph_a = arena[:, 0:4, :].rearrange("p a b -> p (a b)")
        ph_b = arena[:, 4:8, :].rearrange("p a b -> p (a b)")

        bank = [ctx.enter_context(nc.psum_tensor(f"bank{i}", [P, 512], f32)) for i in range(8)]
        tbank = bank[6:8]

        const_loaded = sem("const_loaded")
        blocks_zeroed = sem("blocks_zeroed")
        blocks_loaded = sem("blocks_loaded")
        pool_setup = sem("pool_setup")
        dve_setup = sem("dve_setup")
        act_setup = sem("act_setup")
        x_loaded = [sem(f"x_loaded{r}") for r in range(R)]
        p_loaded = sem("p_loaded")
        chunk_loaded = [sem(f"chunk_loaded{i}") for i in range(SLOTS)]
        chunk_used = sem("chunk_used")
        h_spilled = sem("h_spilled")
        out_stored = sem("out_stored")
        stats_done, aggr_done = sem("stats_done"), sem("aggr_done")
        rstd_done, normed = sem("rstd_done"), sem("normed")
        turned, turned_taken = sem("turned"), sem("turned_taken")
        feat_ready, feat_taken = sem("feat_ready"), sem("feat_taken")
        proj_ready, proj_taken = sem("proj_ready"), sem("proj_taken")
        rope_done = sem("rope_done")
        conv_done = sem("conv_done")
        halo_done = sem("halo_done")
        rg_pool, rg_act, rg_dve = sem("rg_pool"), sem("rg_act"), sem("rg_dve")
        bu_ready, s5_mixed, s5_rotated = sem("bu_ready"), sem("s5_mixed"), sem("s5_rotated")
        s5_scanned, s5_state = sem("s5_scanned"), sem("s5_state")
        y_ready, y_taken = sem("y_ready"), sem("y_taken")
        glu_ready, glu_taken = sem("glu_ready"), sem("glu_taken")
        gl_pool, gl_act, gl_dve = sem("gl_pool"), sem("gl_act"), sem("gl_dve")
        idx_ready, idx_taken, idx_summed = sem("idx_ready"), sem("idx_taken"), sem("idx_summed")
        causal_done = sem("causal_done")
        topk_step = sem("topk_step")
        bias_ready = sem("bias_ready")
        logit_ready, logit_taken = sem("logit_ready"), sem("logit_taken")
        max_ready, exp_done, pv_done = sem("max_ready"), sem("exp_done"), sem("pv_done")
        inv_done, o_normed = sem("inv_done"), sem("o_normed")
        mixed_ready, mixed_taken = sem("mixed_ready"), sem("mixed_taken")
        pp_ready, pp_taken = sem("pp_ready"), sem("pp_taken")
        pg_ready, pg_taken, ple_half, ple_done = sem("pg_ready"), sem("pg_taken"), sem("ple_half"), sem("ple_done")
        up_ready, up_taken = sem("up_ready"), sem("up_taken")
        act_half, act_done = sem("act_half"), sem("act_done")
        down_ready, down_taken, down_added = sem("down_ready"), sem("down_taken"), sem("down_added")
        out_scaled, out_done = sem("out_scaled"), sem("out_done")

        ctx.enter_context(nc.allow_non_contiguous_dma(reason="constants of a few hundred elements"))
        block = ctx.enter_context(nc.Block())

        @block.sync
        def _(sp):
            def chunk_src(c):
                kind = c[0]
                w = w_in[0]
                if kind == "in_cols":
                    return w[:, c[1]:c[1] + 256].rearrange("(k p) n -> p k n", p=P), (KT, 256)
                if kind == "in_rows":
                    return w[c[2] * P:(c[2] + 4) * P, c[1]:c[1] + 512].rearrange("(k p) n -> p k n", p=P), (4, 512)
                if kind == "out":
                    return w_out[0][c[2] * P:(c[2] + 4) * P, c[1] * 512:(c[1] + 1) * 512].rearrange(
                        "(k p) n -> p k n", p=P), (4, 512)
                if kind == "hT":
                    return h_spill[c[1], :, 4 * c[2]:4 * c[2] + 4, :], (4, 512)
                if kind == "ple_p":
                    return ple_w_proj[0][:, c[1] * 512:(c[1] + 1) * 512].rearrange("(k p) n -> p k n", p=P), (2, 512)
                if kind == "ple_g":
                    return ple_w_gate[0][c[2] * P:(c[2] + 4) * P, c[1] * 512:(c[1] + 1) * 512].rearrange(
                        "(k p) n -> p k n", p=P), (4, 512)
                if kind == "down":
                    f, n, half = c[1:]
                    return ffn_w_down[0][f * P:(f + n) * P, half * 512:(half + 1) * 512].rearrange(
                        "(k p) n -> p k n", p=P), (n, 512)

            def load(n):
                c = CHUNKS[n]
                slot = n % SLOTS
                if n >= SLOTS:
                    sp.wait_ge(chunk_used, n - SLOTS + 2)
                if c[0] == "hT":
                    sp.wait_ge(h_spilled, 16 * (c[1] + 1))
                if c[0] == "up":
                    dst = ring[:, slot, :].rearrange("p (k n) -> p k n", k=KT)
                    src = ffn_w_up[0].rearrange("(k p) (h n) -> p k h n", p=P, h=2)
                    f = c[1]
                    for i in (0, 1):
                        sp.dma_start(dst[:, :, i * P:(i + 1) * P], src[:, :, i, f * P:(f + 1) * P]).then_inc(
                            chunk_loaded[slot], 16)
                    return
                src, (k, w) = chunk_src(c)
                dst = ring[:, slot, 0:k * w].rearrange("p (k n) -> p k n", k=k)
                sp.dma_start(dst, src).then_inc(chunk_loaded[slot], 16)

            def x_load(s):
                if s:
                    sp.wait_ge(turned, T_AT["att", s - 1] + attend_t(s - 1))
                for r in range(R):
                    g = row_tile(s, r)
                    sp.dma_start(rows[:, r, :], x[0, g * P:(g + 1) * P, :]).then_inc(x_loaded[r], 16)

            def mix_in(s):
                first = CHUNK_AT["mix", s]
                x_load(s)
                for n in range(first, first + 4):
                    load(n)
                sp.wait_ge(turned_taken, T_AT["mix", s] + KT)
                sp.dma_start(h_spill[s], hT).then_inc(h_spilled, 16)
                for n in range(first + 4, first + 8):
                    load(n)

            def attend(s):
                first = CHUNK_AT["att", s]
                for n in range(first, first + 6):
                    load(n)

            def feed_forward(s):
                if s + 1 < NSB:
                    sp.wait_ge(y_taken, 4 * (s + 2))
                else:
                    sp.wait_ge(turned, T_AT["att", s] + attend_t(s))
                sp.dma_start(p_rows, p[0, 0, s * SB:(s + 1) * SB, :].rearrange("(r p) n -> p r n", p=P)
                             ).then_inc(p_loaded, 16)
                first = CHUNK_AT["ffn", s]
                last = CHUNK_AT["att", s + 1] if s + 1 < NSB else len(CHUNKS)
                for n in range(first, last):
                    load(n)
                for r in range(R):
                    g = row_tile(s, r)
                    sp.wait_ge(out_done, g + 1)
                    sp.dma_start(out[0, g * P:(g + 1) * P, :], rows[:, r, :]).then_inc(out_stored, 16)

            x_load(0)
            sp.dma_start(pos_i[:, :], positions[0].rearrange("(g p) -> p g", p=P)).then_inc(const_loaded, 16)
            for dst, src in ((ln_gb[:, 0, :], ln_emb_g), (ln_gb[:, 1, :], ln_emb_b),
                             (ln_gb[:, 2, :], ln1_g[0]), (ln_gb[:, 3, :], ln1_b[0]),
                             (s5c[:, 0, :], s5_lam_re[0].rearrange("g p -> (g p)")),
                             (s5c[:, 1, :], s5_lam_im[0].rearrange("g p -> (g p)")),
                             (d_col[:, :], s5_d[0]), (bglu_col[:, :], s5_b_glu[0]),
                             (rgc[:, 0, :], rg_conv_b[0]), (rgc[:, 1, :], rg_ba[0]),
                             (rgc[:, 2, :], rg_bx[0]), (rgc[:, 3, :], rg_lam[0])):
                sp.dma_start(dst, src.rearrange("(k p) -> p k", p=P)).then_inc(const_loaded, 16)
            for a in (0, 1):
                sp.dma_start(s5c[64 * a:64 * a + 64, 2, :],
                             s5_log_step[0].rearrange("(i a) -> a i", a=2)[a].partition_broadcast(64)
                             ).then_inc(const_loaded, 16)
            for k in range(RG_CONV):
                sp.dma_start(conv_w[:, :, k], rg_conv_w[0][k].rearrange("(c p) -> p c", p=P)
                             ).then_inc(const_loaded, 16)
            sp.dma_start(w_glu[:, :, :], s5_w_glu[0].rearrange("(k p) n -> p k n", p=P)).then_inc(const_loaded, 16)
            sp.dma_start(w_tail[:, :, :], w_in[0][:, C_KI:N_IN].rearrange("(k p) n -> p k n", p=P)
                         ).then_inc(const_loaded, 16)
            sp.dma_start(g2[:, :], ln2_g[0].partition_broadcast(P)).then_inc(const_loaded, 16)
            sp.dma_start(b2[:, :], ln2_b[0].partition_broadcast(P)).then_inc(const_loaded, 16)
            sp.wait_ge(blocks_zeroed, 4)
            for i, src in enumerate((s5_b_re, s5_b_im)):
                for a in (0, 1):
                    sp.dma_start(
                        blk_b[i][64 * a:64 * a + 64, :].rearrange("p (i a c) -> p i a c", i=NST, a=2)[:, :, a, :],
                        src[0].rearrange("(i a) p c -> a p i c", a=2)[a]).then_inc(blocks_loaded, 16)
            for i, src in enumerate((s5_c_re, s5_c_im)):
                for j in range(4):
                    for a in (0, 1):
                        q = 32 * j + 16 * a
                        sp.dma_start(
                            blk_c[i][q:q + 16, :].rearrange("c (t n) -> c t n", t=2)[:, :, 64 * a:64 * a + 64],
                            src[0].rearrange("(t j a) c p -> j a c t p", j=4, a=2)[j, a]).then_inc(blocks_loaded, 16)
            for i, src in enumerate((rg_wa, rg_wx)):
                for j in range(4):
                    sp.dma_start(w_gates[32 * j:32 * j + 32, i, :, 32 * j:32 * j + 32],
                                 src[0].rearrange("(c j) m n -> j m c n", j=4)[j]).then_inc(blocks_loaded, 16)

            first = CHUNK_AT["mix", 0]
            for n in range(first, first + 4):
                load(n)
            sp.wait_ge(turned_taken, T_AT["mix", 0] + KT)
            sp.dma_start(h_spill[0], hT).then_inc(h_spilled, 16)
            for n in range(first + 4, first + 8):
                load(n)
            attend(0)
            for s in range(NSB):
                if s + 1 < NSB:
                    mix_in(s + 1)
                feed_forward(s)
                if s + 1 < NSB:
                    attend(s + 1)
            sp.wait_ge(out_stored, 16 * SEQ // P)
            sp.wait_ge(h_spilled, 16 * NSB)

        CONSTS = 1 + 12 + 2 + RG_CONV + 2 + 2
        BLOCKS = 4 + 16 + 8

        @block.gpsimd
        def _(pool):
            def norm(call):
                n = NORM[call]
                pool.wait_ge(aggr_done, R * (n + 1))
                pool.tensor_scalar(var_eps[:, :], mv[:, :, 1], EPS, None, ALU.add).then_inc(rstd_done, 1)
                pool.wait_ge(rstd_done, 2 * n + 1)
                pool.tensor_tensor(rstd[:, :], var_eps[:, :], neg_half[:, :], ALU.pow).then_inc(rstd_done, 1)

            def rope(s, j):
                job = 3 * R * s + j
                grp, r = divmod(j, R)
                pool.wait_ge(proj_taken, job + 1)
                if grp:
                    pool.wait_ge(turned, T_AT["mix", s] + KT + (grp - 1) * R + r + 1)
                dst = roped[r]
                if grp == 0:
                    pool.tensor_tensor(dst.rearrange("p (j g d) -> p g j d", j=4, g=2),
                                       rope_a.rearrange("p (g j d) -> p g j d", g=2, j=4),
                                       rope_b.rearrange("p (g j d) -> p g j d", g=2, j=4),
                                       ALU.add).then_inc(rope_done, 1)
                elif grp == 1:
                    pool.tensor_tensor(dst[:, 0:192], rope_a[:, 0:192], rope_b[:, 0:192], ALU.add)
                    pool.tensor_tensor(dst[:, 192:256], rope_a[:, 128:192], rope_b[:, 128:192],
                                       ALU.add).then_inc(rope_done, 1)
                else:
                    pool.tensor_tensor(dst, rope_a, rope_b, ALU.add).then_inc(rope_done, 1)

            def gelu_arg(src, dst, done, at):
                pool.tensor_tensor(dst, src, src, ALU.mult).then_inc(done, 1)
                pool.wait_ge(done, at + 1)
                pool.tensor_scalar(dst, dst, GELU_C, 1.0, ALU.mult, ALU.add).then_inc(done, 1)
                pool.wait_ge(done, at + 2)
                pool.tensor_tensor(dst, dst, src, ALU.mult).then_inc(done, 1)

            def s5_rotate(n):
                m, w = s5_m, s5_w[n % 2]
                pool.wait_ge(s5_mixed, 2 * (n + 1))
                if n >= 2:
                    pool.wait_ge(s5_scanned, 4 * (n - 2) + 2)
                pool.tensor_tensor(w[:, 0, :], m[:, 0, 0, :], m[:, 0, 1, :], ALU.add)
                pool.tensor_tensor(w[:, 1, :], m[:, 1, 0, :], m[:, 1, 1, :], ALU.subtract).then_inc(s5_rotated, 1)

            def s5_finish(n):
                i = n % NST
                xs = s5_x[n % 2]
                pool.wait_ge(s5_scanned, 4 * (n + 1))
                if n >= 2:
                    pool.wait_ge(y_ready, n - 1)
                pool.tensor_tensor(xs[:, 0, :], s5_n[:, 0, 0, :], s5_n[:, 0, 1, :], ALU.subtract)
                pool.tensor_tensor(xs[:, 1, :], s5_n[:, 1, 0, :], s5_n[:, 1, 1, :], ALU.add).then_inc(s5_state, 1)
                pool.wait_ge(s5_state, 2 * n + 1)
                pool.tensor_copy(s5_carry[:, i, :], xs[:, :, TW - 1]).then_inc(s5_state, 1)

            def mix_in(s):
                norm(("emb", s))
                pool.wait_ge(feat_taken, 10 * s + 6)
                gelu_arg(gate_t, gelu_t, rg_pool, 7 * s)
                pool.wait_ge(feat_taken, 10 * s + 10)
                for c in (0, 1):
                    pool.tensor_scalar(ra_t[:, c, :], ra_t[:, c, :], 1.0, rgc[:, 4, c:c + 1],
                                       ALU.add, ALU.mult).then_inc(rg_pool, 1)
                pool.wait_ge(rg_act, 4 * s + 3)
                pool.wait_ge(rg_dve, 6 * s + 2)
                pool.tensor_tensor(conv_t, a_t, a_t, ALU.mult).then_inc(rg_pool, 1)
                pool.wait_ge(rg_act, 4 * s + 4)
                pool.tensor_tensor(ib_t, ib_t, conv_t, ALU.mult).then_inc(rg_pool, 1)
                for t, slot in enumerate(SLOT_LIST):
                    n = t - 1
                    if 0 <= n < STEPS:
                        s5_rotate(STEPS * s + n)
                    if 1 <= n <= STEPS:
                        s5_finish(STEPS * s + n - 1)
                    j = rope_job(slot)
                    if j is not None:
                        rope(s, j)
                pool.wait_ge(y_taken, 4 * (s + 1))
                pool.wait_ge(rg_dve, 6 * s + 3)
                gelu_arg(u_t, gelu_t, gl_pool, 4 * s)
                pool.wait_ge(gl_dve, 2 * (s + 1))
                pool.tensor_scalar(mixT[:, 0:2, :], u_t, 0.25, None, ALU.mult).then_inc(gl_pool, 1)
                done = idx_before(s)
                for r in range(R):
                    g = row_tile(s, r)
                    w, at = width(g), score_at(s, r)
                    if selects(g):
                        done += logit_jobs_of(g)
                        pool.wait_ge(idx_summed, done)
                        pool.affine_select(out=scores[:, at + w - P:at + w], in_=scores[:, at + w - P:at + w],
                                           compare_op=ALU.is_ge, fill=NEG, base=0, pattern=[[-1, P]],
                                           channel_multiplier=1).then_inc(causal_done, 1)
                    else:
                        pool.wait_ge(gl_pool, 4 * (s + 1))
                        pool.wait_ge(rg_dve, 6 * (s + 1))
                        pool.memset(scores[:, at:at + w], 0.0).then_inc(causal_done, 1)
                        pool.wait_ge(causal_done, 2 * g + 1)
                        pool.affine_select(out=scores[:, at + w - P:at + w], in_=scores[:, at + w - P:at + w],
                                           compare_op=ALU.is_ge, fill=-BIG, base=0, pattern=[[-1, P]],
                                           channel_multiplier=1).then_inc(causal_done, 1)

            def attend(s):
                norm(("one", s))

            def feed_forward(s):
                for c in (0, 1):
                    for r in range(R):
                        n = 2 * R * s + R * c + r
                        pool.wait_ge(pp_taken, n + 1)
                        pool.wait_ge(pg_taken, n + 1)
                        pool.tensor_scalar(evac_b[n % 2], evac_b[n % 2], 1.0, None, ALU.add).then_inc(ple_half, 1)
                        pool.wait_ge(ple_half, n + 1)
                        pool.tensor_tensor(rows[:, r, c * 512:(c + 1) * 512], evac_b[n % 2], half_pp[r],
                                           ALU.mult).then_inc(ple_done, 1)
                for half in (0, 1):
                    for i in range(HALF_F):
                        f = NF * s + half * HALF_F + i
                        pool.wait_ge(up_taken, 3 * (f + 1))
                        pool.tensor_scalar(tanh_b[f % 2], tanh_b[f % 2], 1.0, None, ALU.add).then_inc(act_half, 1)
                        pool.wait_ge(act_half, 2 * f + 1)
                        pool.tensor_tensor(tanh_b[f % 2], tanh_b[f % 2], gate_b[f % 2], ALU.mult
                                           ).then_inc(act_half, 1)
                        if i == 0 and half == 0 and s + 1 < NSB:
                            pool.wait_ge(h_spilled, 16 * (s + 2))
                            pool.wait_ge(idx_summed, idx_before(s + 2))
                        if i == 0 and half == 1:
                            pool.wait_ge(down_ready, DOWN_JOBS * s + DOWN_JOBS // 2)
                        pool.wait_ge(act_half, 2 * f + 2)
                        pool.tensor_tensor(act[:, i, :], tanh_b[f % 2], up_b[f % 2], ALU.mult).then_inc(act_done, 1)
                    for c in (0, 1):
                        for r in range(R):
                            n = DOWN_JOBS * s + 2 * R * half + R * c + r
                            pool.wait_ge(down_taken, n + 1)
                            if half:
                                pool.wait_ge(down_added, n - 2 * R + 1)
                            dst = rows[:, r, c * 512:(c + 1) * 512]
                            pool.tensor_tensor(dst, dst, evac_b[n % 2], ALU.add).then_inc(down_added, 1)
                norm(("two", s))
                for r in range(R):
                    g = row_tile(s, r)
                    pool.wait_ge(normed, R * NORM["two", s] + r + 1)
                    pool.tensor_tensor(rows[:, r, :], rows[:, r, :], g2[:, :], ALU.mult).then_inc(out_scaled, 1)
                    pool.wait_ge(out_scaled, g + 1)
                    pool.tensor_tensor(rows[:, r, :], rows[:, r, :], b2[:, :], ALU.add).then_inc(out_done, 1)

            for i in (0, 1):
                pool.memset(blk_b[i], 0.0).then_inc(blocks_zeroed, 1)
            pool.memset(scores[:, 4096:4608], 0.0).then_inc(blocks_zeroed, 1)
            pool.memset(w_gates[:, :, :, :], 0.0).then_inc(blocks_zeroed, 1)
            pool.memset(ident[:, :], 0.0).then_inc(pool_setup, 1)
            pool.wait_ge(pool_setup, 1)
            pool.affine_select(out=ident[:, :], in_=ident[:, :], compare_op=ALU.not_equal, fill=1.0,
                               base=0, pattern=[[-1, P]], channel_multiplier=1).then_inc(pool_setup, 1)
            pool.wait_ge(pool_setup, 2)
            pool.tensor_scalar(alpha_i[:, :], ident[:, :], ALPHA, None, ALU.mult)
            pool.memset(neg_half[:, :], -0.5)
            pool.memset(s5_carry[:, :, :], 0.0)
            pool.memset(halo[:, :, :], 0.0)
            pool.memset(rg_carry[:, :], 0.0)
            for i in range(32):
                pool.memset(inv_f[:, i:i + 1], float(np.float32(10000.0) ** np.float32(-2.0 * i / HD)))
            pool.memset(rstd[:, :], 0.0).then_inc(pool_setup, 1)

            mix_in(0)
            attend(0)
            for s in range(NSB):
                if s + 1 < NSB:
                    mix_in(s + 1)
                feed_forward(s)
                if s + 1 < NSB:
                    attend(s + 1)

        @block.scalar
        def _(scalar):
            def take(t, dst, src, **kw):
                scalar.wait_ge(turned, t + 1)
                scalar.activation(dst, src, **kw).then_inc(turned_taken, 1)

            def norm_turned(t0, dst, g_row):
                for k in range(KT):
                    t = t0 + k
                    take(t, dst[:, k, :], tbank[t % 2][:, :], func=ACT.Identity,
                         scale=ln_gb[:, g_row, k:k + 1], bias=ln_gb[:, g_row + 1, k:k + 1])

            def mix_in(s):
                t0 = T_AT["mix", s]
                norm_turned(t0, hT, 0)
                for m in range(6):
                    n = 10 * s + m
                    src = bank[4 + n % 2][:, :]
                    if m == 0:
                        scalar.activation(xr_t[:, :, 0:3], halo[:, :, :], ACT.Copy).then_inc(halo_done, 1)
                    scalar.wait_ge(feat_ready, n + 1)
                    dst = (xr_t[:, 0, 3:515], xr_t[:, 1, 3:515], u_t[:, 0, :], u_t[:, 1, :],
                           gate_t[:, 0, :], gate_t[:, 1, :])[m]
                    scalar.activation(dst, src, ACT.Copy).then_inc(feat_taken, 1)
                    if m == 1:
                        scalar.wait_ge(feat_taken, n + 1)
                        scalar.wait_ge(halo_done, 2 * s + 1)
                        scalar.activation(halo[:, :, :], xr_t[:, :, 512:515], ACT.Copy).then_inc(halo_done, 1)
                for m in range(4):
                    n = 10 * s + 6 + m
                    kind, c = divmod(m, 2)
                    scalar.wait_ge(feat_ready, n + 1)
                    scalar.activation((ra_t, ib_t)[kind][:, c, :], bank[4 + n % 2][:, :], ACT.Tanh, scale=0.5,
                                      bias=rgc[:, 5 + kind, c:c + 1]).then_inc(feat_taken, 1)
                scalar.wait_ge(rg_pool, 7 * s + 3)
                scalar.activation(gelu_t, gelu_t, ACT.Tanh, scale=GELU_K).then_inc(rg_act, 1)
                scalar.wait_ge(rg_pool, 7 * s + 5)
                scalar.wait_ge(conv_done, 8 * (s + 1))
                scalar.wait_ge(halo_done, 2 * s + 2)
                scalar.activation(a_t, ra_t, ACT.Exp).then_inc(rg_act, 1)
                scalar.wait_ge(rg_act, 4 * s + 2)
                scalar.activation(ra_t, ra_t, ACT.Tanh, scale=-1.0).then_inc(rg_act, 1)
                scalar.wait_ge(rg_dve, 6 * s + 3)
                scalar.activation(conv_t, conv_t, ACT.Sqrt, scale=0.25).then_inc(rg_act, 1)
                for slot in SLOT_LIST:
                    j = transposed_in(slot)
                    if j is None:
                        continue
                    grp, r = divmod(j, R)
                    g = row_tile(s, r)
                    t = t0 + KT + j
                    src = tbank[t % 2][:, :].rearrange("p (j q) -> p j q", j=4)
                    if grp == 0:
                        take(t, qT[:, :, r * P:(r + 1) * P], src, func=ACT.Copy, scale=HD ** -0.5)
                    elif grp == 1:
                        take(t, keysT[:, :, g * P:(g + 1) * P], src[:, 0:2, :], func=ACT.Copy)
                    else:
                        take(t, qiT[:, :, r * P:(r + 1) * P], src, func=ACT.Copy)
                scalar.wait_ge(gl_pool, 4 * s + 3)
                scalar.activation(gelu_t, gelu_t, ACT.Tanh, scale=GELU_K).then_inc(gl_act, 1)
                for c in (0, 1):
                    scalar.wait_ge(glu_ready, 2 * s + c + 1)
                    scalar.activation(gelu_t[:, c, :], bank[4 + c][:, :], ACT.Tanh, scale=0.25,
                                      bias=s5c[:, 20 + c, 0:1]).then_inc(glu_taken, 1)
                n = idx_before(s)
                for r, h, a, w in idx_jobs(s):
                    scalar.wait_ge(idx_ready, n + 1)
                    if n >= 3:
                        scalar.wait_ge(idx_summed, n - 2)
                    scalar.activation(relu_buf[:, n % 3, 0:w], bank[n % 4][:, 0:w], ACT.Relu
                                      ).then_inc(idx_taken, 1)
                    n += 1

            def attend(s):
                if s:
                    scalar.wait_ge(act_done, NF * s)

                def out_turned(g):
                    t = t_out(g)
                    r = g % R
                    take(t, mixT[:, 4:8, r * P:(r + 1) * P],
                         tbank[t % 2][:, :].rearrange("p (j q) -> p j q", j=4), func=ACT.Copy)

                for r in range(R):
                    g = row_tile(s, r)
                    w = width(g)
                    for h in range(HEADS):
                        n = HEADS * g + h
                        scalar.wait_ge(max_ready, n + 1)
                        if h == 0 and g >= 2:
                            scalar.wait_ge(inv_done, g - 1)
                        scalar.activation(prob[n % 2][:, 0:w], prob[n % 2][:, 0:w], ACT.Exp,
                                          bias=neg_max[:, n % 2:n % 2 + 1],
                                          accum_out=row_sum[:, g % 2, h:h + 1]).then_inc(exp_done, 1)
                        t = t_attn(g, h)
                        if n >= 2:
                            scalar.wait_ge(pv_done, n - 1)
                        for a, pw in pieces(w):
                            take(t, probT[n % 2][:, a:a + pw], tbank[t % 2][:, 0:pw], func=ACT.Copy)
                            t += 1
                        if h == 0 and r:
                            out_turned(g - 1)
                out_turned(row_tile(s, R - 1))
                for c in (0, 1):
                    for r in range(R):
                        n = 2 * R * s + R * c + r
                        scalar.wait_ge(mixed_ready, n + 1)
                        if s and c == 0:
                            scalar.wait_ge(out_stored, 16 * R * s)
                        scalar.activation(rows[:, r, c * 512:(c + 1) * 512], bank[r][:, :], ACT.Copy
                                          ).then_inc(mixed_taken, 1)
                norm_turned(T_AT["att", s] + attend_t(s) - KT, h1T, 2)

            def feed_forward(s):
                for k in range(D_PLE // P):
                    t = T_AT["ffn", s] + k
                    take(t, pT[:, k, :], tbank[t % 2][:, :], func=ACT.Copy)
                for c in (0, 1):
                    for r in range(R):
                        n = 2 * R * s + R * c + r
                        scalar.wait_ge(pp_ready, n + 1)
                        if c:
                            scalar.wait_ge(ple_done, n - R + 1)
                        scalar.activation(half_pp[r], bank[4 + n % 2][:, :], ACT.Copy, scale=0.5
                                          ).then_inc(pp_taken, 1)
                    for r in range(R):
                        n = 2 * R * s + R * c + r
                        scalar.wait_ge(pg_ready, n + 1)
                        if n >= 2:
                            scalar.wait_ge(ple_done, n - 1)
                        scalar.activation(evac_b[n % 2], bank[r][:, :], ACT.Tanh, scale=0.5).then_inc(pg_taken, 1)
                scalar.wait_ge(ple_done, 2 * R * (s + 1))
                for half in (0, 1):
                    for i in range(HALF_F):
                        f = NF * s + half * HALF_F + i
                        gate, up = bank[4 + 2 * (f % 2)], bank[5 + 2 * (f % 2)]
                        scalar.wait_ge(up_ready, 2 * f + 1)
                        if f >= 2:
                            scalar.wait_ge(act_done, f - 1)
                        scalar.activation(tanh_b[f % 2], gate[:, :], ACT.Tanh, scale=0.5).then_inc(up_taken, 1)
                        scalar.activation(gate_b[f % 2], gate[:, :], ACT.Copy).then_inc(up_taken, 1)
                        scalar.wait_ge(up_ready, 2 * f + 2)
                        scalar.activation(up_b[f % 2], up[:, :], ACT.Copy, scale=0.5).then_inc(up_taken, 1)
                    for c in (0, 1):
                        for r in range(R):
                            n = DOWN_JOBS * s + 2 * R * half + R * c + r
                            scalar.wait_ge(down_ready, n + 1)
                            if n >= 2:
                                scalar.wait_ge(down_added, n - 1)
                            scalar.activation(evac_b[n % 2], bank[r][:, :], ACT.Copy).then_inc(down_taken, 1)

            scalar.wait_ge(const_loaded, 16 * CONSTS)
            scalar.activation(s5c[:, 3, :], s5c[:, 2, :], ACT.Exp).then_inc(act_setup, 1)
            scalar.activation(rgc[:, 7, :], rgc[:, 3, :], ACT.Abs).then_inc(act_setup, 1)
            scalar.wait_ge(act_setup, 2)
            scalar.activation(rgc[:, 8, :], rgc[:, 7, :], ACT.Exp, scale=-1.0).then_inc(act_setup, 1)
            scalar.wait_ge(dve_setup, 1)
            scalar.activation(s5c[:, 5, :], s5c[:, 4, :], ACT.Exp).then_inc(act_setup, 1)
            scalar.wait_ge(dve_setup, SETUP_ANGLES)
            scalar.activation(s5c[:, 8, :], s5c[:, 6, :], ACT.Sin)
            scalar.activation(s5c[:, 9, :], s5c[:, 7, :], ACT.Sin)
            scalar.activation(sin_t[:, :, 1, :], tmp_a[:, 0:512].rearrange("p (g f) -> p g f", g=16), ACT.Sin)
            scalar.activation(cos_t[:, :, :], tmp_b[:, 0:512].rearrange("p (g f) -> p g f", g=16), ACT.Sin)
            scalar.activation(sin_t[:, :, 0, :], tmp_a[:, 0:512].rearrange("p (g f) -> p g f", g=16), ACT.Sin,
                              scale=-1.0).then_inc(act_setup, 1)
            take(0, bT[:, :, :, :], tbank[0][:, :].rearrange("p (m t q) -> p m t q", m=2, t=2), func=ACT.Copy)
            scalar.wait_ge(turned, 2)
            scalar.activation(cT[:, 0, :, :], tbank[1][:, 0:256].rearrange("p (i c) -> p i c", c=32), ACT.Copy)
            scalar.activation(cT[:, 1, :, :], tbank[1][:, 256:512].rearrange("p (i c) -> p i c", c=32), ACT.Copy,
                              scale=-1.0).then_inc(turned_taken, 1)

            scalar.wait_ge(dve_setup, SETUP_PHASES)
            mix_in(0)
            attend(0)
            for s in range(NSB):
                if s + 1 < NSB:
                    mix_in(s + 1)
                feed_forward(s)
                if s + 1 < NSB:
                    attend(s + 1)

        @block.vector
        def _(dve):
            setup_n = [0]

            def link(ins):
                setup_n[0] += 1
                ins.then_inc(dve_setup, 1)
                dve.wait_ge(dve_setup, setup_n[0])

            def norm(call, ready):
                n = NORM[call]
                for r in range(R):
                    ready(r)
                    dve.bn_stats(stats[:, r, 0, :], rows[:, r, 0:512])
                    dve.bn_stats(stats[:, r, 1, :], rows[:, r, 512:1024]).then_inc(stats_done, 1)
                for r in range(R):
                    dve.wait_ge(stats_done, R * n + r + 1)
                    dve.bn_aggr(mv[:, r, :], stats[:, r, :, :].rearrange("p a b -> p (a b)")).then_inc(aggr_done, 1)
                dve.wait_ge(rstd_done, 2 * (n + 1))
                for r in range(R):
                    dve.tensor_scalar(rows[:, r, :], rows[:, r, :], mv[:, r, 0:1], rstd[:, r:r + 1],
                                      ALU.subtract, ALU.mult).then_inc(normed, 1)

            def rope(s, j):
                job = 3 * R * s + j
                grp, r = divmod(j, R)
                g = row_tile(s, r)
                src = bank[r]
                dve.wait_ge(proj_ready, job + 1)
                if j:
                    dve.wait_ge(rope_done, job)

                def products(a, heads, at):
                    view = src[:, a:a + heads * HD].rearrange("p (h c f) -> p h c f", h=heads, c=2)
                    to = [t[:, at:at + heads * HD].rearrange("p (h c f) -> p h c f", h=heads, c=2)
                          for t in (rope_a, rope_b)]
                    cs = cos_t[:, g, :].unsqueeze(1).unsqueeze(1).to_broadcast([P, heads, 2, 32])
                    sn = sin_t[:, g, :, :].unsqueeze(1).to_broadcast([P, heads, 2, 32])
                    dve.tensor_tensor(to[0], view, cs, ALU.mult)
                    return dve.tensor_tensor(to[1], view[:, :, ::-1, :], sn, ALU.mult)

                if grp != 1:
                    products(0, HEADS, 0).then_inc(proj_taken, 1)
                    return
                products(0, KVH, 0)
                products(256, 1, P)
                dve.tensor_copy(vals[:, g, :], src[:, P:2 * P])
                dve.tensor_scalar(w_idx[:, r, :], src[:, 320:328], (HEADS * HD) ** -0.5, None,
                                  ALU.mult).then_inc(proj_taken, 1)

            def s5_mix(n):
                i = n % NST
                dve.wait_ge(bu_ready, n + 1)
                if n:
                    dve.wait_ge(s5_rotated, n)
                bu = bank[4][:, :].rearrange("p (c t) -> p c t", c=2)
                dve.tensor_tensor(s5_m[:, 0, :, :], bu, phase[:, i, :, :], ALU.mult).then_inc(s5_mixed, 1)
                dve.tensor_tensor(s5_m[:, 1, :, :], bu[:, ::-1, :], phase[:, i, :, :], ALU.mult
                                  ).then_inc(s5_mixed, 1)

            def s5_scan(n):
                i = n % NST
                mag = s5c[:, 5, i:i + 1].to_broadcast([P, TW])
                dve.wait_ge(s5_rotated, n + 1)
                if n >= NST:
                    dve.wait_ge(s5_state, 2 * (n - NST + 1))
                if n:
                    dve.wait_ge(s5_scanned, 4 * n)
                for c in (0, 1):
                    dve.tensor_tensor_scan(s5_z[:, c, :], mag, s5_w[n % 2][:, c, :], s5_carry[:, i, c:c + 1],
                                           ALU.mult, ALU.add).then_inc(s5_scanned, 1)
                dve.wait_ge(s5_scanned, 4 * n + 2)
                if n:
                    dve.wait_ge(s5_state, 2 * n - 1)
                dve.tensor_tensor(s5_n[:, 0, :, :], s5_z[:, :, :], phase[:, i, :, :], ALU.mult
                                  ).then_inc(s5_scanned, 1)
                dve.tensor_tensor(s5_n[:, 1, :, :], s5_z[:, ::-1, :], phase[:, i, :, :], ALU.mult
                                  ).then_inc(s5_scanned, 1)

            def y_take(s, sub):
                n = 4 * s + 2 * sub
                dve.wait_ge(y_ready, STEPS * s + NST * (sub + 1))
                for c in (0, 1):
                    part = u_t[:, c, sub * TW:(sub + 1) * TW]
                    dve.scalar_tensor_tensor(part, part, d_col[:, c:c + 1], bank[5][:, c * TW:(c + 1) * TW],
                                             ALU.mult, ALU.add).then_inc(y_taken, 1)

            def mix_in(s):
                norm(("emb", s), lambda r: dve.wait_ge(x_loaded[r], 16 * (s + 1)))
                n = 8 * s
                dve.wait_ge(feat_taken, 10 * s + 2)
                dve.wait_ge(halo_done, 2 * s + 1)
                for k in range(RG_CONV):
                    for c in (0, 1):
                        src = xr_t[:, c, k:k + 512]
                        if k == 0:
                            ins = dve.tensor_scalar(conv_t[:, c, :], src, conv_w[:, c, 0:1], rgc[:, 0, c:c + 1],
                                                    ALU.mult, ALU.add)
                        else:
                            dve.wait_ge(conv_done, n - 1)
                            ins = dve.scalar_tensor_tensor(conv_t[:, c, :], src, conv_w[:, c, k:k + 1],
                                                           conv_t[:, c, :], ALU.mult, ALU.add)
                        ins.then_inc(conv_done, 1)
                        n += 1
                dve.wait_ge(feat_taken, 10 * (s + 1))
                dve.scalar_tensor_tensor(ib_t, ib_t, 1.0, conv_t, ALU.add, ALU.mult).then_inc(rg_dve, 1)
                dve.wait_ge(rg_act, 4 * s + 1)
                dve.scalar_tensor_tensor(gate_t, gelu_t, 1.0, gate_t, ALU.add, ALU.mult).then_inc(rg_dve, 1)
                dve.wait_ge(rg_pool, 7 * s + 6)
                dve.wait_ge(rg_act, 4 * s + 3)
                dve.scalar_tensor_tensor(conv_t, conv_t, 1.0, ra_t, ALU.add, ALU.mult).then_inc(rg_dve, 1)
                dve.wait_ge(rg_pool, 7 * (s + 1))
                dve.wait_ge(rg_dve, 6 * s + 3)
                for c in (0, 1):
                    dve.tensor_tensor_scan(ra_t[:, c, :], a_t[:, c, :], ib_t[:, c, :], rg_carry[:, c:c + 1],
                                           ALU.mult, ALU.add).then_inc(rg_dve, 1)
                dve.wait_ge(rg_dve, 6 * s + 5)
                dve.tensor_copy(rg_carry[:, :], ra_t[:, :, 511])
                dve.scalar_tensor_tensor(mixT[:, 2:4, :], ra_t, 0.5, gate_t, ALU.mult, ALU.mult
                                         ).then_inc(rg_dve, 1)
                for t, slot in enumerate(SLOT_LIST):
                    n = t - 1
                    if 0 <= n < STEPS:
                        s5_mix(STEPS * s + n)
                    if 1 <= n <= STEPS:
                        s5_scan(STEPS * s + n - 1)
                    if n == NST + 1:
                        y_take(s, 0)
                    if n == STEPS + 1:
                        y_take(s, 1)
                    j = rope_job(slot)
                    if j is not None:
                        rope(s, j)
                dve.wait_ge(gl_act, s + 1)
                dve.scalar_tensor_tensor(u_t, gelu_t, 1.0, u_t, ALU.add, ALU.mult).then_inc(gl_dve, 1)
                dve.wait_ge(glu_taken, 2 * (s + 1))
                dve.wait_ge(gl_dve, 2 * s + 1)
                dve.scalar_tensor_tensor(u_t, gelu_t, 1.0, u_t, ALU.add, ALU.mult).then_inc(gl_dve, 1)
                n = idx_before(s)
                if idx_jobs(s):
                    dve.wait_ge(gl_pool, 4 * (s + 1))
                for r, h, a, w in idx_jobs(s):
                    part = scores[:, score_at(s, r) + a:score_at(s, r) + a + w]
                    src = relu_buf[:, n % 3, 0:w]
                    wh = w_idx[:, r, h:h + 1]
                    dve.wait_ge(idx_taken, n + 1)
                    if h == 0:
                        if n == idx_before(s):
                            dve.wait_ge(rg_dve, 6 * (s + 1))
                        dve.tensor_scalar(part, src, wh, None, ALU.mult).then_inc(idx_summed, 1)
                    else:
                        dve.wait_ge(idx_summed, n + 1 - len(pieces(width(row_tile(s, r)))))
                        dve.scalar_tensor_tensor(part, src, wh, part, ALU.mult, ALU.add).then_inc(idx_summed, 1)
                    n += 1
                for pair in ((0, 1), (2, 3)):
                    if not selects(row_tile(s, pair[0])):
                        continue
                    sel = [scores[:, score_at(s, r):score_at(s, r) + width(row_tile(s, r))] for r in pair]
                    edge = causal_before(row_tile(s, pair[1]) + 1)
                    dve.wait_ge(causal_done, edge)
                    per = 4
                    with dve.Fori(0, TOPK // 8 // per):
                        for u in range(per):
                            for i in (0, 1):
                                if u:
                                    dve.wait_ge(topk_step, 4 * (u - 1) + 3 + i)
                                dve.max(top8[:, i, :], sel[i]).then_inc(topk_step, 1)
                            for i in (0, 1):
                                dve.wait_ge(topk_step, 4 * u + 1 + i)
                                dve.match_replace(sel[i], top8[:, i, :], sel[i], MARK).then_inc(topk_step, 1)
                        dve.wait_ge(topk_step, 4 * per)
                        dve.sem_clear(topk_step)
                    for i in (0, 1):
                        dve.tensor_scalar(sel[i], sel[i], MARK, -BIG, ALU.not_equal, ALU.mult
                                          ).then_inc(bias_ready, 1)

            def causal_before(g):
                return sum(1 if selects(i) else 2 for i in range(g))

            def attend(s):
                def logits(g, h):
                    n = HEADS * g + h
                    w, at = width(g), score_at(*divmod(g, R))
                    job = logits_before(g) + h * len(pieces(w))
                    if n >= 2:
                        g2_, h2_ = divmod(n - 2, HEADS)
                        dve.wait_ge(turned, t_attn(g2_, h2_) + len(pieces(width(g2_))))
                    for i, (a, pw) in enumerate(pieces(w)):
                        dve.wait_ge(logit_ready, job + 1)
                        dve.tensor_tensor_reduce(prob[n % 2][:, a:a + pw], bank[job % 4][:, 0:pw],
                                                 scores[:, at + a:at + a + pw], 1.0, NEG, ALU.add, ALU.max,
                                                 accum_out=part_max[:, n % 2, i:i + 1]).then_inc(logit_taken, 1)
                        job += 1
                    dve.wait_ge(logit_taken, job)
                    if n >= 2:
                        dve.wait_ge(exp_done, n - 1)
                    dve.tensor_reduce(neg_max[:, n % 2:n % 2 + 1], part_max[:, n % 2, 0:len(pieces(w))], X_AXIS,
                                      ALU.max, negate=True).then_inc(max_ready, 1)

                def normalise(g):
                    dve.wait_ge(exp_done, HEADS * (g + 1))
                    dve.reciprocal(inv_sum[:, g % 2, :], row_sum[:, g % 2, :]).then_inc(inv_done, 1)
                    dve.wait_ge(pv_done, HEADS * (g + 1))
                    dve.wait_ge(inv_done, g + 1)
                    if g % R >= 2:
                        dve.wait_ge(turned, t_out(g - 2) + 1)
                    dve.tensor_tensor(o_rows[g % 2].rearrange("p (h d) -> p h d", h=HEADS),
                                      bank[4 + g % 2][:, :].rearrange("p (h d) -> p h d", h=HEADS),
                                      inv_sum[:, g % 2, :].unsqueeze(2).to_broadcast([P, HEADS, HD]),
                                      ALU.mult).then_inc(o_normed, 1)

                dve.wait_ge(causal_done, causal_before(row_tile(s, R)))
                dve.wait_ge(bias_ready, R * s + R - TOPK // P)
                if s:
                    dve.wait_ge(act_done, NF * s)
                for r in range(R):
                    g = row_tile(s, r)
                    logits(g, 0)
                    if r:
                        normalise(g - 1)
                    for h in range(1, HEADS):
                        logits(g, h)
                normalise(row_tile(s, R - 1))
                norm(("one", s), lambda r: dve.wait_ge(mixed_taken, 2 * R * s + R + r + 1))

            def feed_forward(s):
                norm(("two", s), lambda r: dve.wait_ge(down_added, DOWN_JOBS * s + DOWN_JOBS - R + r + 1))

            def reduce_angle(sin_arg, cos_arg, angle, tmp):
                c1, c2, c3 = split_two_pi()
                link(dve.tensor_scalar(tmp, angle, 1 / TWO_PI, MAGIC, ALU.mult, ALU.add))
                link(dve.tensor_scalar(tmp, tmp, MAGIC, None, ALU.subtract))
                for part in (c1, c2, c3):
                    link(dve.scalar_tensor_tensor(angle, tmp, -part, angle, ALU.mult, ALU.add))
                link(dve.tensor_scalar(sin_arg, angle, 3.1415925, -3.1415925, ALU.min, ALU.max))
                link(dve.tensor_scalar(tmp, sin_arg, -1.0, None, ALU.mult))
                link(dve.tensor_tensor(tmp, tmp, sin_arg, ALU.max))
                link(dve.tensor_scalar(cos_arg, tmp, -1.0, math.pi / 2, ALU.mult, ALU.add))

            def k_(i):
                return s5c[:, i, :]

            lr, li, step, mag = k_(0), k_(1), k_(3), k_(5)
            dve.wait_ge(const_loaded, 16 * CONSTS)
            dve.wait_ge(act_setup, 1)
            link(dve.tensor_tensor(k_(4), lr, step, ALU.mult))
            link(dve.tensor_tensor(k_(10), li, step, ALU.mult))
            link(dve.tensor_copy(pos_f[:, :], pos_i[:, :]))
            reduce_angle(k_(6), k_(7), k_(10), k_(11))
            ang = tmp_c[:, 0:512]
            dve.wait_ge(pool_setup, 3)
            link(dve.tensor_tensor(ang.rearrange("p (g f) -> p g f", g=16),
                                   pos_f[:, :].unsqueeze(2).to_broadcast([P, 16, 32]),
                                   inv_f[:, :].unsqueeze(1).to_broadcast([P, 16, 32]), ALU.mult))
            reduce_angle(tmp_a[:, 0:512], tmp_b[:, 0:512], ang, tmp_d[:, 0:512])
            assert setup_n[0] == SETUP_ANGLES
            dve.wait_ge(act_setup, 3)
            y, z, z2, acc = rgc[:, 8, :], rgc[:, 9, :], rgc[:, 10, :], rgc[:, 11, :]
            link(dve.tensor_scalar(z, y, 2.0, None, ALU.add))
            link(dve.reciprocal(z, z))
            link(dve.tensor_tensor(z, z, y, ALU.mult))
            link(dve.tensor_tensor(z2, z, z, ALU.mult))
            link(dve.tensor_scalar(acc, z2, 1 / 17, 1 / 15, ALU.mult, ALU.add))
            for n in (13, 11, 9, 7, 5, 3, 1):
                link(dve.tensor_tensor(acc, acc, z2, ALU.mult))
                link(dve.tensor_scalar(acc, acc, 1 / n, None, ALU.add))
            link(dve.tensor_tensor(acc, acc, z, ALU.mult))
            link(dve.tensor_scalar(z, rgc[:, 3, :], -1.0, 0.0, ALU.mult, ALU.max))
            link(dve.scalar_tensor_tensor(acc, acc, 2.0, z, ALU.mult, ALU.add))
            link(dve.tensor_scalar(rgc[:, 4, :], acc, -4.0, None, ALU.mult))
            link(dve.tensor_scalar(rgc[:, 5, :], rgc[:, 1, :], 0.5, None, ALU.mult))
            link(dve.tensor_scalar(rgc[:, 6, :], rgc[:, 2, :], 0.5, None, ALU.mult))
            link(dve.tensor_scalar(s5c[:, 20:22, 0], bglu_col[:, :], 0.5, None, ALU.mult))
            dve.wait_ge(act_setup, 5)
            ar, ai, nr, den, cr, ci, t1, t2 = (k_(i) for i in (12, 13, 14, 15, 16, 17, 18, 19))
            link(dve.tensor_tensor(ar, mag, k_(9), ALU.mult))
            link(dve.tensor_tensor(ai, mag, k_(8), ALU.mult))
            link(dve.tensor_tensor(den, lr, lr, ALU.mult))
            link(dve.tensor_tensor(t1, li, li, ALU.mult))
            link(dve.tensor_tensor(den, den, t1, ALU.add))
            link(dve.reciprocal(den, den))
            link(dve.tensor_scalar(nr, ar, -1.0, None, ALU.add))
            link(dve.tensor_tensor(t1, nr, lr, ALU.mult))
            link(dve.tensor_tensor(t2, ai, li, ALU.mult))
            link(dve.tensor_tensor(t1, t1, t2, ALU.add))
            link(dve.tensor_tensor(cr, t1, den, ALU.mult))
            link(dve.tensor_tensor(t1, ai, lr, ALU.mult))
            link(dve.tensor_tensor(t2, nr, li, ALU.mult))
            link(dve.tensor_tensor(t1, t1, t2, ALU.subtract))
            link(dve.tensor_tensor(ci, t1, den, ALU.mult))
            dve.wait_ge(blocks_loaded, 16 * BLOCKS)
            b4 = [t.rearrange("p (i c) -> p i c", c=32) for t in blk_b]
            crb = cr.unsqueeze(2).to_broadcast([P, NST, 32])
            cib = ci.unsqueeze(2).to_broadcast([P, NST, 32])
            s4 = scores[:, 5120:5376].rearrange("p (i c) -> p i c", c=32)
            link(dve.tensor_tensor(b4[2], b4[0], crb, ALU.mult))
            link(dve.tensor_tensor(s4, b4[1], cib, ALU.mult))
            link(dve.tensor_tensor(b4[2], b4[2], s4, ALU.subtract))
            link(dve.tensor_tensor(b4[3], b4[1], crb, ALU.mult))
            link(dve.tensor_tensor(s4, b4[0], cib, ALU.mult))
            link(dve.tensor_tensor(b4[3], b4[3], s4, ALU.add))
            assert setup_n[0] == SETUP_MATRICES
            link(dve.tensor_copy(phase[:, :, 0, 0], k_(9)))
            link(dve.tensor_copy(phase[:, :, 1, 0], k_(8)))
            m = 1
            while m < TW:
                a = ph_a[:, 0:NST * m].rearrange("p (i t) -> p i t", i=NST)
                b = ph_b[:, 0:NST * m].rearrange("p (i t) -> p i t", i=NST)
                lo = [phase[:, :, c, 0:m] for c in (0, 1)]
                by = [phase[:, :, c, m - 1:m].to_broadcast([P, NST, m]) for c in (0, 1)]
                link(dve.tensor_tensor(a, lo[0], by[0], ALU.mult))
                link(dve.tensor_tensor(b, lo[1], by[1], ALU.mult))
                link(dve.tensor_tensor(phase[:, :, 0, m:2 * m], a, b, ALU.subtract))
                link(dve.tensor_tensor(a, lo[0], by[1], ALU.mult))
                link(dve.tensor_tensor(b, lo[1], by[0], ALU.mult))
                link(dve.tensor_tensor(phase[:, :, 1, m:2 * m], a, b, ALU.add))
                m *= 2
            assert setup_n[0] == SETUP_PHASES

            mix_in(0)
            attend(0)
            for s in range(NSB):
                if s + 1 < NSB:
                    mix_in(s + 1)
                feed_forward(s)
                if s + 1 < NSB:
                    attend(s + 1)

        @block.tensor
        def _(pe):
            def arrived(n, k, w):
                pe.wait_ge(chunk_loaded[n % SLOTS], loads_until(n))
                return ring[:, n % SLOTS, 0:k * w].rearrange("p (k n) -> p k n", k=k)

            def loads_until(n):
                return sum(32 if CHUNKS[i][0] == "up" else 16 for i in range(n % SLOTS, n + 1, SLOTS))

            def turn(t, blocks):
                if t >= 2:
                    pe.wait_ge(turned_taken, t - 1)
                for i, src in enumerate(blocks):
                    ins = pe.transpose(tbank[t % 2][:, i * P:(i + 1) * P], src, ident[:, :])
                ins.then_inc(turned, 1)

            def norm_turn(call, t0):
                pe.wait_ge(normed, R * (NORM[call] + 1))
                for k in range(KT):
                    turn(t0 + k, [rows[:, r, k * P:(k + 1) * P] for r in range(R)])

            def s5_in(n):
                i = n % NST
                c, j = divmod(i, 4)
                sub = (n % STEPS) // NST
                if n:
                    pe.wait_ge(s5_mixed, 2 * n)
                rhs = u_t[32 * j:32 * j + 32, c, sub * TW:(sub + 1) * TW]
                for m in (0, 1):
                    ins = pe.matmul(bank[4][:, m * TW:(m + 1) * TW], bT[32 * j:32 * j + 32, m, c, :], rhs,
                                    start=True, stop=True)
                ins.then_inc(bu_ready, 1)

            def s5_out(n):
                i = n % NST
                c, j = divmod(i, 4)
                q = n // NST
                pe.wait_ge(s5_state, 2 * n + 1)
                if i == 0 and q:
                    pe.wait_ge(y_taken, 2 * q)
                for m in (0, 1):
                    ins = pe.matmul(bank[5][32 * j:32 * j + 32, c * TW:(c + 1) * TW], cT[:, m, i, :],
                                    s5_x[n % 2][:, m, :], start=(m == 0), stop=(m == 1))
                ins.then_inc(y_ready, 1)

            def mix_in(s):
                t0 = T_AT["mix", s]
                norm_turn(("emb", s), t0)
                c0 = CHUNK_AT["mix", s]
                for m in range(6):
                    n = 10 * s + m
                    if m % 2 == 0:
                        w = arrived(c0 + m // 2, KT, 256)
                    if m == 0 and s:
                        pe.wait_ge(o_normed, R * s)
                    if m >= 2:
                        pe.wait_ge(feat_taken, n - 1)
                    for k in range(KT):
                        if m == 0:
                            pe.wait_ge(turned_taken, t0 + k + 1)
                        ins = pe.matmul(bank[4 + n % 2][:, :], w[:, k, (m % 2) * P:(m % 2 + 1) * P], hT[:, k, :],
                                        start=(k == 0), stop=(k == KT - 1))
                        if m % 2 == 0 and k == 0:
                            ins.then_inc(chunk_used, 1)
                    ins.then_inc(feat_ready, 1)
                pe.wait_ge(conv_done, 8 * (s + 1))
                for m in range(4):
                    n = 10 * s + 6 + m
                    kind, c = divmod(m, 2)
                    pe.wait_ge(feat_taken, n - 1)
                    pe.matmul(bank[4 + n % 2][:, :], w_gates[:, kind, c, :], conv_t[:, c, :], start=True,
                              stop=True).then_inc(feat_ready, 1)
                pe.wait_ge(feat_taken, 10 * (s + 1))
                for t, (kind, half, r) in enumerate(SLOT_LIST):
                    if kind == "kv":
                        job = 3 * R * s + R + r
                        w = arrived(c0 + 5, KT, 256)
                        pe.wait_ge(proj_taken, job - 3)
                        for tile, at, n_ in ((w, 0, 256), (w_tail, 256, N_IN - C_KI)):
                            for k in range(KT):
                                ins = pe.matmul(bank[r][:, at:at + n_], hT[:, k, r * P:(r + 1) * P], tile[:, k, :],
                                                start=(k == 0), stop=(k == KT - 1))
                                if r == 0 and at == 0 and k == 0:
                                    ins.then_inc(chunk_used, 1)
                        ins.then_inc(proj_ready, 1)
                    elif kind in GROUP_OF:
                        grp = GROUP_OF[kind]
                        job = 3 * R * s + R * grp + r
                        c = c0 + (3 if kind == "q" else 6) + half
                        w = arrived(c, 4, 512)
                        if half == 0:
                            if kind == "qi":
                                pe.wait_ge(proj_taken, job - 3)
                            elif s and r == 0:
                                pe.wait_ge(mixed_taken, 2 * R * s)
                        for k in range(4):
                            ins = pe.matmul(bank[r][:, :], hT[:, 4 * half + k, r * P:(r + 1) * P], w[:, k, :],
                                            start=(half == 0 and k == 0), stop=(half == 1 and k == 3))
                            if r == 0 and k == 0:
                                ins.then_inc(chunk_used, 1)
                        if half:
                            ins.then_inc(proj_ready, 1)
                    n = t - 1
                    if 0 <= n < STEPS:
                        s5_in(STEPS * s + n)
                    if 2 <= n < STEPS + 2:
                        s5_out(STEPS * s + n - 2)
                    j = transposed_in((kind, half, r))
                    if j is not None:
                        pe.wait_ge(rope_done, 3 * R * s + j + 1)
                        blocks = 2 if R <= j < 2 * R else 4
                        turn(t0 + KT + j, [roped[j % R][:, i * P:(i + 1) * P] for i in range(blocks)])
                pe.wait_ge(gl_dve, 2 * s + 1)
                pe.wait_ge(y_taken, 4 * (s + 1))
                for c in (0, 1):
                    for k in (0, 1):
                        ins = pe.matmul(bank[4 + c][:, :], w_glu[:, k, c * P:(c + 1) * P], u_t[:, k, :],
                                        start=(k == 0), stop=(k == 1))
                    ins.then_inc(glu_ready, 1)
                pe.wait_ge(proj_taken, 3 * R * (s + 1))
                pe.wait_ge(turned_taken, t0 + MIX_T)
                n = idx_before(s)
                for r, h, a, w in idx_jobs(s):
                    if n >= 4:
                        pe.wait_ge(idx_taken, n - 3)
                    q = 64 * (h % 2)
                    pe.matmul(bank[n % 4][:, 0:w], qiT[q:q + 64, h // 2, r * P:(r + 1) * P],
                              keysT[q:q + 64, 1, a:a + w], start=True, stop=True).then_inc(idx_ready, 1)
                    n += 1

            def attend(s):
                def logits(g, h):
                    q = 64 * (h // 4)
                    r = g % R
                    job = logits_before(g) + h * len(pieces(width(g)))
                    for a, w in pieces(width(g)):
                        if job >= 4:
                            pe.wait_ge(logit_taken, job - 3)
                        pe.matmul(bank[job % 4][:, 0:w], qT[q:q + 64, h % 4, r * P:(r + 1) * P],
                                  keysT[q:q + 64, 0, a:a + w], start=True, stop=True).then_inc(logit_ready, 1)
                        job += 1

                def values(g, h):
                    n = HEADS * g + h
                    t = t_attn(g, h)
                    kv = h // 4
                    parts = pieces(width(g))
                    pe.wait_ge(exp_done, n + 1)
                    if h == 0 and g >= 2:
                        pe.wait_ge(o_normed, g - 1)

                    def turn_part(i):
                        a, w = parts[i]
                        turn(t + i, [prob[n % 2][:, a + b:a + b + P] for b in range(0, w, P)])

                    turn_part(0)
                    for i, (a, w) in enumerate(parts):
                        if i + 1 < len(parts):
                            turn_part(i + 1)
                        pe.wait_ge(turned_taken, t + i + 1)
                        for b in range(0, w, P):
                            kt = (a + b) // P
                            ins = pe.matmul(bank[4 + g % 2][:, h * HD:(h + 1) * HD], probT[n % 2][:, a + b:a + b + P],
                                            vals[:, kt, kv * HD:(kv + 1) * HD], start=(kt == 0), stop=(kt == g))
                    ins.then_inc(pv_done, 1)

                def out_turn(g):
                    pe.wait_ge(o_normed, g + 1)
                    turn(t_out(g), [o_rows[g % 2][:, j * P:(j + 1) * P] for j in range(4)])

                pe.wait_ge(idx_taken, idx_before(s + 1))
                if s:
                    pe.wait_ge(down_taken, DOWN_JOBS * s)
                    pe.wait_ge(up_taken, 3 * NF * s)
                else:
                    pe.wait_ge(proj_taken, 3 * R)
                    pe.wait_ge(glu_taken, 2)
                order = [(row_tile(s, r), h) for r in range(R) for h in range(HEADS)]
                logits(*order[0])
                for i, (g, h) in enumerate(order):
                    if i + 1 < len(order):
                        logits(*order[i + 1])
                    values(g, h)
                    if h == 0 and g % R:
                        out_turn(g - 1)
                out_turn(row_tile(s, R - 1))
                c0 = CHUNK_AT["att", s]
                pe.wait_ge(logit_taken, logits_before(row_tile(s, R)))
                pe.wait_ge(turned_taken, t_out(row_tile(s, R - 1)) + 1)
                pe.wait_ge(rg_dve, 6 * (s + 1))
                pe.wait_ge(gl_pool, 4 * (s + 1))
                for c in (0, 1):
                    for part in (0, 1):
                        w = arrived(c0 + 3 * c + part, 4, 512)
                        for r in range(R):
                            if c and part == 0:
                                pe.wait_ge(mixed_taken, 2 * R * s + r + 1)
                            for k in range(4):
                                ins = pe.matmul(bank[r][:, :], mixT[:, 4 * part + k, r * P:(r + 1) * P], w[:, k, :],
                                                start=(part == 0 and k == 0), stop=False)
                                if r == 0 and k == 0:
                                    ins.then_inc(chunk_used, 1)
                    w = arrived(c0 + 3 * c + 2, 4, 512)
                    for r in range(R):
                        for k in range(4):
                            ins = pe.matmul(bank[r][:, k * P:(k + 1) * P], w[:, k, r * P:(r + 1) * P],
                                            alpha_i[:, :], start=False, stop=(k == 3))
                            if r == 0 and k == 0:
                                ins.then_inc(chunk_used, 1)
                        ins.then_inc(mixed_ready, 1)
                norm_turn(("one", s), T_AT["att", s] + attend_t(s) - KT)

            def feed_forward(s):
                pe.wait_ge(p_loaded, 16 * (s + 1))
                for k in range(D_PLE // P):
                    turn(T_AT["ffn", s] + k, [p_rows[:, r, k * P:(k + 1) * P] for r in range(R)])
                pe.wait_ge(turned_taken, T_AT["ffn", s] + D_PLE // P)
                c0 = CHUNK_AT["ffn", s]
                if s + 1 < NSB:
                    pe.wait_ge(glu_taken, 2 * (s + 2))
                    pe.wait_ge(idx_taken, idx_before(s + 2))
                else:
                    pe.wait_ge(o_normed, R * (s + 1))
                    pe.wait_ge(mixed_taken, 2 * R * (s + 1))
                for c in (0, 1):
                    w = arrived(c0 + 3 * c, 2, 512)
                    for r in range(R):
                        n = 2 * R * s + R * c + r
                        if n % (2 * R) >= 2:
                            pe.wait_ge(pp_taken, n - 1)
                        for k in (0, 1):
                            ins = pe.matmul(bank[4 + n % 2][:, :], pT[:, k, r * P:(r + 1) * P], w[:, k, :],
                                            start=(k == 0), stop=(k == 1))
                            if r == 0 and k == 0:
                                ins.then_inc(chunk_used, 1)
                        ins.then_inc(pp_ready, 1)
                    for part in (0, 1):
                        w = arrived(c0 + 3 * c + 1 + part, 4, 512)
                        for r in range(R):
                            n = 2 * R * s + R * c + r
                            if c and part == 0:
                                pe.wait_ge(pg_taken, n - R + 1)
                            for k in range(4):
                                ins = pe.matmul(bank[r][:, :], h1T[:, 4 * part + k, r * P:(r + 1) * P], w[:, k, :],
                                                start=(part == 0 and k == 0), stop=(part == 1 and k == 3))
                                if r == 0 and k == 0:
                                    ins.then_inc(chunk_used, 1)
                            if part:
                                ins.then_inc(pg_ready, 1)
                pe.wait_ge(pp_taken, 2 * R * (s + 1))
                c0 += 6
                for half in (0, 1):
                    for i in range(HALF_F):
                        f = NF * s + half * HALF_F + i
                        w = arrived(c0, KT, 256)
                        if f % NF >= 2:
                            pe.wait_ge(up_taken, 3 * (f - 1))
                        for m in (0, 1):
                            for k in range(KT):
                                ins = pe.matmul(bank[4 + 2 * (f % 2) + m][:, :], w[:, k, m * P:(m + 1) * P],
                                                h1T[:, k, :], start=(k == 0), stop=(k == KT - 1))
                                if m == 0 and k == 0:
                                    ins.then_inc(chunk_used, 1)
                            ins.then_inc(up_ready, 1)
                        c0 += 1
                    for c in (0, 1):
                        for a in range(0, HALF_F, 4):
                            nf = min(4, HALF_F - a)
                            w = arrived(c0, nf, 512)
                            for r in range(R):
                                n = DOWN_JOBS * s + 2 * R * half + R * c + r
                                if a == 0:
                                    if half == 0 and c == 0:
                                        pe.wait_ge(pg_taken, 2 * R * (s + 1))
                                    else:
                                        pe.wait_ge(down_taken, n - R + 1)
                                for k in range(nf):
                                    if r == 0 and c == 0:
                                        pe.wait_ge(act_done, NF * s + half * HALF_F + a + k + 1)
                                    last = half == 0 and a + k == HALF_F - 1
                                    ins = pe.matmul(bank[r][:, :], act[:, a + k, r * P:(r + 1) * P], w[:, k, :],
                                                    start=(a + k == 0), stop=last)
                                    if r == 0 and k == 0:
                                        ins.then_inc(chunk_used, 1)
                                if last:
                                    ins.then_inc(down_ready, 1)
                                if half and a + nf == HALF_F:
                                    for k in range(4):
                                        ins = pe.matmul(bank[r][:, k * P:(k + 1) * P],
                                                        h1T[:, 4 * c + k, r * P:(r + 1) * P], alpha_i[:, :],
                                                        start=False, stop=(k == 3))
                                    ins.then_inc(down_ready, 1)
                            c0 += 1

            pe.wait_ge(pool_setup, 3)
            pe.wait_ge(dve_setup, SETUP_MATRICES)
            turn(0, [blk_b[2 + m][:, c * P:(c + 1) * P] for m in (0, 1) for c in (0, 1)])
            turn(1, [blk_c[m][:, c * P:(c + 1) * P] for m in (0, 1) for c in (0, 1)])
            pe.wait_ge(turned_taken, 2)

            mix_in(0)
            attend(0)
            for s in range(NSB):
                if s + 1 < NSB:
                    mix_in(s + 1)
                feed_forward(s)
                if s + 1 < NSB:
                    attend(s + 1)


_INS = ["x", "p", "positions", "ln_emb_g", "ln_emb_b", "w_in",
        "s5_lam_re", "s5_lam_im", "s5_log_step", "s5_b_re", "s5_b_im", "s5_c_re", "s5_c_im",
        "s5_d", "s5_w_glu", "s5_b_glu",
        "rg_conv_w", "rg_conv_b", "rg_wa", "rg_ba", "rg_wx", "rg_bx", "rg_lam",
        "w_out", "ln1_g", "ln1_b", "ffn_w_up", "ffn_w_down", "ple_w_gate", "ple_w_proj",
        "ln2_g", "ln2_b"]


def kernel(**inputs):
    import concourse.bacc as bacc
    from concourse.bass_utils import run_bass_kernel_spmd

    nc = bacc.Bacc("TRN2", target_bir_lowering=False, num_devices=1, dynamic_dma_scratch_size=1024)
    arrays, args = {}, []
    for name in _INS:
        a = np.ascontiguousarray(inputs[name])
        arrays[f"in_{name}_dram"] = a
        args.append(nc.dram_tensor(f"in_{name}_dram", a.shape, mybir.dt.from_np(a.dtype), kind="ExternalInput").ap())
    out = nc.dram_tensor("out_0_dram", (1, SEQ, D), mybir.dt.float32, kind="ExternalOutput").ap()
    h_spill = nc.dram_tensor("h_spill", (NSB, P, KT, SB), mybir.dt.float32, kind="Internal").ap()
    trunk_kernel(nc, *args, out, h_spill)
    r = run_bass_kernel_spmd(nc, [arrays], core_ids=[0])
    return r.results[0]["out_0_dram"]
```

```python
import math
from contextlib import ExitStack

import numpy as np
import concourse.bass as bass
from concourse import mybir

P = 128
D = 1024
SEQ = 2048
SB = 512
NSB = SEQ // SB
R = SB // P
KT = D // P
D_S5, S5_GROUP, S5_GROUPS, S5_STATE = 256, 16, 16, 64
NST = S5_GROUPS * S5_STATE // P
TW = 256
SUBS = SB // TW
STEPS = SUBS * NST
RG_CONV = 4
HEADS, HD, KVH = 8, 64, 2
TOPK = 256
N_IN = 2120
D_FF = 2816
NF = D_FF // P
PARTS = [(0, 2)] + [(f, 4) for f in range(2, NF, 4)]
ACTS = 5
D_PLE = 256
ALPHA = 2.0 ** 0.25
EPS = 1e-5
C_XRG, C_GRG, C_Q, C_K, C_QI, C_KI = 256, 512, 768, 1280, 1536, 2048
UNIT = 512
SLOTS = 3
CH = 1024
MARK = -3.4e38
NEG = -3.0e38
BIG = 1.0e30
TWO_PI = 2 * math.pi
MAGIC = 12582912.0
GELU_C, GELU_K = 0.044715, math.sqrt(2 / math.pi)


def split_two_pi():
    a = np.float32(6.28125)
    b = np.float32(np.floor((TWO_PI - float(a)) * 2 ** 20) / 2 ** 20)
    return float(a), float(b), float(np.float32(TWO_PI - float(a) - float(b)))


def row_tile(s, r):
    return s * R + r


def width(g):
    return (g + 1) * P


def score_at(s, r):
    return sum(width(row_tile(s, i)) for i in range(r))


def pieces(w):
    return [(a, min(UNIT, w - a)) for a in range(0, w, UNIT)]


def selects(g):
    return (g + 1) * P > TOPK


SETUP_ANGLES = 22
SETUP_MATRICES = SETUP_ANGLES + 47
SETUP_PHASES = SETUP_MATRICES + 2 + 6 * 8


def attend_t(s):
    return sum(HEADS * len(pieces(width(row_tile(s, r)))) + 1 for r in range(R))


def t_start():
    order = [("emb", 0), ("setup", 0), ("mix", 0), ("att", 0)]
    for s in range(NSB):
        if s + 1 < NSB:
            order += [("emb", s + 1), ("one", s), ("mix", s + 1), ("ffn", s), ("att", s + 1)]
        else:
            order += [("one", s), ("ffn", s)]
    t, at = 0, {}
    for kind, s in order:
        at[kind, s] = t
        t += {"emb": KT, "one": KT, "setup": 2, "mix": 4 * R, "ffn": D_PLE // P}.get(kind) or attend_t(s)
    return at


T_AT = t_start()


def norm_calls():
    order = [("emb", 0)]
    for s in range(NSB):
        if s + 1 < NSB:
            order.append(("emb", s + 1))
        order.append(("one", s))
        order.append(("two", s))
    return {call: n for n, call in enumerate(order)}


NORM = norm_calls()


def idx_jobs(s):
    return [(r, h, a, w) for r in range(R) if selects(row_tile(s, r))
            for h in range(HEADS) for a, w in pieces(width(row_tile(s, r)))]


def before(count, s):
    return sum(count(i) for i in range(s))


def idx_before(s):
    return before(lambda i: len(idx_jobs(i)), s)


def logit_jobs_of(g):
    return HEADS * len(pieces(width(g)))


def logits_before(g):
    return before(logit_jobs_of, g)


def t_attn(g, h):
    s, r = divmod(g, R)
    t = T_AT["att", s]
    for i in range(r):
        t += HEADS * len(pieces(width(row_tile(s, i)))) + 1
    n = len(pieces(width(g)))
    late = r > 0
    return t - late + h * n + (late and h >= 1)


def t_out(g):
    s, r = divmod(g, R)
    if r + 1 < R:
        return t_attn(g + 1, 0) + len(pieces(width(g + 1)))
    return T_AT["att", s] + attend_t(s) - 1


GROUP_OF = {"q": 0, "kv": 1, "qi": 2}
GROUP_CHUNKS = {"q": 4, "kv": 2, "qi": 4}
SLOT_LIST = ([(kind, c, r) for kind in ("q", "kv", "qi") for c in range(GROUP_CHUNKS[kind]) for r in range(R)]
             + [("end", 0, r) for r in range(R)])


def rope_job(slot):
    kind, c, r = slot
    if kind != "end" and c == GROUP_CHUNKS[kind] - 1:
        return GROUP_OF[kind] * R + r
    return None


def turned_banks(j):
    return [j] if j < 2 * R else [2 * j - 2 * R, 2 * j - 2 * R + 1]


def lower_heads(i):
    return [(0, 1, 4)] if i == 0 else [(0, 5, 3), (3, 0, 1)]


def transposed_in(slot):
    kind, c, r = slot
    if kind == "q" or c:
        return None
    return {"kv": 0, "qi": R, "end": 2 * R}[kind] + r


def s5_step_of(t):
    n, odd = divmod(t, 2)
    return None if odd or n > STEPS + 1 else n


def ffn_steps():
    steps, f = [], 0
    for p, (first, count) in enumerate(PARTS):
        while f < min(first + count + 1, NF):
            steps.append(("up", f))
            f += 1
        steps.append(("down", p))
    return steps


FFN_STEPS = ffn_steps()


def chunk_list():
    def mix(s):
        return ([("cols", c) for at in (C_XRG, 0, C_GRG) for c in (at, at + P)]
                + [("rows", C_Q, k) for k in range(0, KT, 2)]
                + [("kv", k) for k in (0, 4)]
                + [("rows", C_QI, k) for k in range(0, KT, 2)])

    def att(s):
        return [x for c in (0, 1) for x in [("out", c, k) for k in range(0, KT, 2)]
                + [("hT", s, 4 * c + k) for k in (0, 2)]]

    def ffn(s):
        got = [x for c in (0, 1) for x in [("ple_p", c)] + [("ple_g", c, k) for k in range(0, KT, 2)]]
        for kind, i in FFN_STEPS:
            if kind == "up":
                got += [("up", m, i) for m in (0, 1)]
            else:
                first, count = PARTS[i]
                got += [("down", first + a, c) for c in (0, 1) for a in range(0, count, 2)]
        return got

    order, start = [], {}

    def put(kind, s, part):
        start[kind, s] = len(order)
        order.extend(part)

    put("mix", 0, mix(0))
    put("att", 0, att(0))
    for s in range(NSB):
        if s + 1 < NSB:
            put("mix", s + 1, mix(s + 1))
        put("ffn", s, ffn(s))
        if s + 1 < NSB:
            put("att", s + 1, att(s + 1))
    return order, start


CHUNKS, CHUNK_AT = chunk_list()
FFN_CHUNKS = 2 * 5 + 2 * NF + NF
IS_SPLIT = [c[0] in ("out", "ple_g", "up", "down") for c in CHUNKS]
SPLITS = [n for n, split in enumerate(IS_SPLIT) if split]
SPLIT_OF = {n: m for m, n in enumerate(SPLITS)}


def splits_until(n):
    return sum(IS_SPLIT[:n + 1])


def part_of(f):
    return next(p for p, (first, count) in enumerate(PARTS) if f < first + count)


DOWN_JOBS = len(PARTS) * 2 * R


def trunk_kernel(nc, x, p, positions, ln_emb_g, ln_emb_b, w_in,
                 s5_lam_re, s5_lam_im, s5_log_step, s5_b_re, s5_b_im, s5_c_re, s5_c_im,
                 s5_d, s5_w_glu, s5_b_glu,
                 rg_conv_w, rg_conv_b, rg_wa, rg_ba, rg_wx, rg_bx, rg_lam,
                 w_out, ln1_g, ln1_b, ffn_w_up, ffn_w_down, ple_w_gate, ple_w_proj,
                 ln2_g, ln2_b, out, h_spill, phase_spill):
    f32 = mybir.dt.float32
    f32r = mybir.dt.float32r
    i32 = mybir.dt.int32
    ALU = mybir.AluOpType
    ACT = mybir.ActivationFunctionType
    X_AXIS = mybir.AxisListType.X

    with ExitStack() as ctx:
        def sb(name, shape, dt=f32):
            return ctx.enter_context(nc.sbuf_tensor(name, shape, dt))

        def sb_pair(name, shape):
            with nc.sbuf_tensor(name, shape, f32) as whole:
                pass
            return whole, sb(name + "_parts", shape, f32r)

        def sem(name):
            return ctx.enter_context(nc.semaphore(name))

        ring = sb("ring", [P, SLOTS, CH])
        pairs = sb("pairs", [P, SLOTS, 2, CH], f32r)
        arena, arena_parts = sb_pair("arena", [P, 18, UNIT])
        rows = sb("rows", [P, R, D])
        scores = sb("scores", [P, 58 * P])
        qT = sb("qT", [P, 4, SB])
        mixT, mixT_parts = sb_pair("mixT", [P, KT, SB])
        keysT = sb("keysT", [P, SEQ])
        idx_keys = sb("idx_keys", [P, 2, SEQ], f32r)
        vals = sb("vals", [P, SEQ // P, P])
        phase, phase_parts = sb_pair("phase", [P, NST, 2, TW])
        work = sb("work", [P, 7, UNIT])
        ident = sb("ident", [P, P])
        alpha_i = sb("alpha_i", [P, P])
        ones = sb("ones", [P, HD])
        bT = sb("bT", [P, 2, 2, P])
        cT = sb("cT", [P, 2, NST, 32])
        w_glu = sb("w_glu", [P, 2, D_S5])
        w_gates = sb("w_gates", [P, 2, 2, P])
        w_tail = sb("w_tail", [P, KT, N_IN - C_KI])
        cos_t = sb("cos_t", [P, SEQ // P, 32])
        sin_t = sb("sin_t", [P, SEQ // P, 2, 32])
        ln_gb = sb("ln_gb", [P, 4, KT])
        s5c = sb("s5c", [P, 24, NST])
        s5_carry = sb("s5_carry", [P, NST, 2])
        d_col = sb("d_col", [P, 2])
        bglu_col = sb("bglu_col", [P, 2])
        conv_w = sb("conv_w", [P, 2, RG_CONV])
        rgc = sb("rgc", [P, 12, 2])
        halo = sb("halo", [P, 2, RG_CONV - 1])
        rg_carry = sb("rg_carry", [P, 2])
        pos_i = sb("pos_i", [P, SEQ // P], i32)
        pos_f = sb("pos_f", [P, SEQ // P])
        inv_f = sb("inv_f", [P, 32])
        stats = sb("stats", [P, R, 2, 6])
        mv = sb("mv", [P, R, 2])
        var_eps = sb("var_eps", [P, R])
        rstd = sb("rstd", [P, R])
        neg_half = sb("neg_half", [P, R])
        w_idx = sb("w_idx", [P, R, HEADS])
        top8 = sb("top8", [P, 2, 8])
        part_max = sb("part_max", [P, 2, 4])
        neg_max = sb("neg_max", [P, 2])
        row_sum = sb("row_sum", [P, 2, HEADS])
        inv_sum = sb("inv_sum", [P, 2, HEADS])

        hT = arena[:, 0:KT, :]
        h1T = arena[:, KT:2 * KT, :]
        h1_pair = [arena_parts[:, 0:KT, :], arena_parts[:, KT:2 * KT, :]]
        spare = phase_parts[:, :, :, :].rearrange("p i c t -> p i (c t)")
        act_pair = [[spare[:, 2 * i + m, :] if i < 4 else arena_parts[:, 16 + m, :] for i in range(ACTS)]
                    for m in (0, 1)]
        mix_pair = [[spare[:, 4 * m + k, :] if k < 4 else mixT_parts[:, k - 4 * m, :] for k in range(KT)]
                    for m in (0, 1)]
        relu_buf = [arena[:, 16, :], arena[:, 17, :], work[:, 6, :]]
        prob = [arena[:, 4 * i:4 * i + 4, :].rearrange("p a b -> p (a b)") for i in (0, 1)]
        probT = [arena[:, 8 + 4 * i:12 + 4 * i, :].rearrange("p a b -> p (a b)") for i in (0, 1)]
        idx_qT = pairs[:, 0:2, :, :].rearrange("p s m n -> p (s m n)").rearrange("p (h q) -> p h q", h=HEADS)
        gb2 = mixT[:, 4:8, :].rearrange("p (a b) n -> p a (b n)", a=2)
        u_t = scores[:, 0:1024].rearrange("p (a b) -> p a b", a=2)
        xr_t = scores[:, 1024:1024 + 2 * 515].rearrange("p (a b) -> p a b", a=2)
        o_ = 1024 + 2 * 515
        gate_t, gelu_t, conv_t, ra_t, ib_t = (
            scores[:, o_ + 1024 * i:o_ + 1024 * (i + 1)].rearrange("p (a b) -> p a b", a=2) for i in range(5))
        a_t = xr_t[:, :, 3:515]
        next_rows = scores[:, 0:R * D].rearrange("p (r d) -> p r d", r=R)
        rope_a, rope_b = rows[:, 0, 0:512], rows[:, 0, 512:1024]
        roped = [rows[:, 1, 0:512], rows[:, 1, 512:1024], rows[:, 2, 0:512], rows[:, 2, 512:1024]]
        s5_m = rows[:, 3, :].rearrange("p (m c t) -> p m c t", m=2, c=2)
        s5_w = [work[:, i, :].rearrange("p (c t) -> p c t", c=2) for i in (0, 1)]
        s5_z = work[:, 2, :].rearrange("p (c t) -> p c t", c=2)
        s5_n = work[:, 3:5, :].rearrange("p m (c t) -> p m c t", c=2)
        s5_x = [work[:, 5 + i, :].rearrange("p (c t) -> p c t", c=2) for i in (0, 1)]
        p_rows = work[:, 0:2, :].rearrange("p a (b c) -> p (a b) c", b=2)
        pT = work[:, 4:6, :]
        half_pp = [mixT[:, 4 + r, :] for r in range(R)]
        tanh_b = [mixT[:, 4, :], mixT[:, 5, :]]
        gate_b = [mixT[:, 6, :], mixT[:, 7, :]]
        up_b = [work[:, 0, :], work[:, 1, :]]
        evac_b = [work[:, 2, :], work[:, 3, :]]
        down_b = [work[:, i, :] for i in (2, 3, 4, 5)]
        o_scale = [work[:, 0, :], work[:, 1, :]]
        o_turned = [work[:, 2, :], work[:, 3, :]]
        inv_diag = work[:, 4:6, :].rearrange("p a (b q) -> p (a b) q", q=P)
        setup = mixT[:, 4:8, :].rearrange("p a b -> p (a b)")
        blk_b = [setup[:, 256 * i:256 * (i + 1)] for i in range(4)]
        blk_c = [setup[:, 1024 + 256 * i:1024 + 256 * (i + 1)] for i in range(2)]
        tmp_a, tmp_b, tmp_c, tmp_d = (mixT[:, i, :] for i in range(4))
        ph_a = arena[:, 8:12, :].rearrange("p a b -> p (a b)")
        ph_b = arena[:, 12:16, :].rearrange("p a b -> p (a b)")

        bank = [ctx.enter_context(nc.psum_tensor(f"bank{i}", [P, 512], f32)) for i in range(8)]
        tbank = bank[6:8]

        const_loaded = sem("const_loaded")
        blocks_zeroed = sem("blocks_zeroed")
        blocks_loaded = sem("blocks_loaded")
        pool_setup = sem("pool_setup")
        dve_setup = sem("dve_setup")
        act_setup = sem("act_setup")
        ln_loaded = sem("ln_loaded")
        x_loaded = [sem(f"x_loaded{r}") for r in range(R)]
        p_loaded = sem("p_loaded")
        chunk_loaded = [sem(f"chunk_loaded{i}") for i in range(SLOTS)]
        chunk_used = sem("chunk_used")
        split_high, split_low = sem("split_high"), sem("split_low")
        h_spilled = sem("h_spilled")
        phase_spilled, phase_loaded = sem("phase_spilled"), sem("phase_loaded")
        mix_high, mix_low = sem("mix_high"), sem("mix_low")
        h1_split = sem("h1_split")
        turned_high = sem("turned_high")
        gb2_loaded = sem("gb2_loaded")
        out_stored = sem("out_stored")
        stats_done, aggr_done = sem("stats_done"), sem("aggr_done")
        rstd_done, normed = sem("rstd_done"), sem("normed")
        turned, turned_taken = sem("turned"), sem("turned_taken")
        feat_ready, feat_taken = sem("feat_ready"), sem("feat_taken")
        proj_ready, proj_taken = sem("proj_ready"), sem("proj_taken")
        rope_done = sem("rope_done")
        conv_done = sem("conv_done")
        halo_done = sem("halo_done")
        rg_pool, rg_act, rg_dve = sem("rg_pool"), sem("rg_act"), sem("rg_dve")
        bu_ready, s5_mixed, s5_rotated = sem("bu_ready"), sem("s5_mixed"), sem("s5_rotated")
        s5_scanned, s5_state = sem("s5_scanned"), sem("s5_state")
        y_ready, y_taken = sem("y_ready"), sem("y_taken")
        glu_ready, glu_taken = sem("glu_ready"), sem("glu_taken")
        gl_pool, gl_act, gl_dve = sem("gl_pool"), sem("gl_act"), sem("gl_dve")
        idx_ready, idx_taken, idx_summed = sem("idx_ready"), sem("idx_taken"), sem("idx_summed")
        causal_done = sem("causal_done")
        topk_step = sem("topk_step")
        bias_ready = sem("bias_ready")
        logit_ready, logit_taken = sem("logit_ready"), sem("logit_taken")
        max_ready, exp_done, pv_done = sem("max_ready"), sem("exp_done"), sem("pv_done")
        inv_done, diag_done, o_normed = sem("inv_done"), sem("diag_done"), sem("o_normed")
        mixed_ready, mixed_taken = sem("mixed_ready"), sem("mixed_taken")
        pp_ready, pp_taken = sem("pp_ready"), sem("pp_taken")
        pg_ready, pg_taken, ple_half, ple_done = sem("pg_ready"), sem("pg_taken"), sem("ple_half"), sem("ple_done")
        up_ready, up_taken = sem("up_ready"), sem("up_taken")
        act_one, act_half, act_high, act_done = sem("act_one"), sem("act_half"), sem("act_high"), sem("act_done")
        down_ready, down_taken, down_added = sem("down_ready"), sem("down_taken"), sem("down_added")
        out_scaled, out_done = sem("out_scaled"), sem("out_done")

        ctx.enter_context(nc.allow_non_contiguous_dma(reason="constants of a few hundred elements"))
        block = ctx.enter_context(nc.Block())

        @block.sync
        def _(sp):
            def chunk_src(c):
                kind = c[0]
                w = w_in[0]
                if kind == "cols":
                    return w[:, c[1]:c[1] + P].rearrange("(k p) n -> p k n", p=P), (KT, P)
                if kind == "rows":
                    return w[c[2] * P:(c[2] + 2) * P, c[1]:c[1] + 512].rearrange("(k p) n -> p k n", p=P), (2, 512)
                if kind == "kv":
                    return w[c[1] * P:(c[1] + 4) * P, C_K:C_QI].rearrange("(k p) n -> p k n", p=P), (4, 256)
                if kind == "hT":
                    return h_spill[c[1], :, c[2]:c[2] + 2, :], (2, 512)
                if kind == "ple_p":
                    return ple_w_proj[0][:, c[1] * 512:(c[1] + 1) * 512].rearrange("(k p) n -> p k n", p=P), (2, 512)
                if kind == "up":
                    return ffn_w_up[0][:, c[1] * D_FF + c[2] * P:c[1] * D_FF + (c[2] + 1) * P].rearrange(
                        "(k p) n -> p k n", p=P), (KT, P)
                if kind == "down":
                    return ffn_w_down[0][c[1] * P:(c[1] + 2) * P, c[2] * 512:(c[2] + 1) * 512].rearrange(
                        "(k p) n -> p k n", p=P), (2, 512)
                w = {"out": w_out, "ple_g": ple_w_gate}[kind][0]
                return w[c[2] * P:(c[2] + 2) * P, c[1] * 512:(c[1] + 1) * 512].rearrange(
                    "(k p) n -> p k n", p=P), (2, 512)

            def load(n):
                c = CHUNKS[n]
                slot = n % SLOTS
                if n >= SLOTS:
                    last = n - SLOTS
                    if IS_SPLIT[last]:
                        sp.wait_ge(split_low, splits_until(last))
                    else:
                        sp.wait_ge(chunk_used, last + 2)
                if c[0] == "hT":
                    sp.wait_ge(h_spilled, 16 * (c[1] + 1))
                src, (k, w) = chunk_src(c)
                dst = ring[:, slot, 0:k * w].rearrange("p (k n) -> p k n", k=k)
                sp.dma_start(dst, src).then_inc(chunk_loaded[slot], 16)

            def load_gb2(s):
                sp.wait_ge(act_done, NF * (s + 1))
                for i, src in enumerate((ln2_g, ln2_b)):
                    sp.dma_start(gb2[:, i, :], src[0].partition_broadcast(P)).then_inc(gb2_loaded, 16)

            def x_load(s):
                if s:
                    sp.wait_ge(logit_taken, logits_before(row_tile(s, 0)))
                for r in range(R):
                    g = row_tile(s, r)
                    sp.dma_start((next_rows if s else rows)[:, r, :], x[0, g * P:(g + 1) * P, :]
                                 ).then_inc(x_loaded[r], 16)

            def spill_h(s):
                sp.wait_ge(turned_taken, T_AT["emb", s] + KT)
                sp.dma_start(h_spill[s], hT).then_inc(h_spilled, 16)

            def mix_in(s):
                first = CHUNK_AT["mix", s]
                sp.wait_ge(mixed_ready, 2 * R * s)
                sp.wait_ge(phase_spilled, 16)
                sp.dma_start(phase[:, :, :, :], phase_spill).then_inc(phase_loaded, 16)
                for n in range(first, first + 6):
                    load(n)
                spill_h(s)
                for n in range(first + 6, first + 16):
                    load(n)

            def attend(s):
                first = CHUNK_AT["att", s]
                for n in range(first + (SLOTS if s else 0), first + 12):
                    if n == first + 5 and s + 1 < NSB:
                        x_load(s + 1)
                    load(n)

            def feed_forward(s):
                first = CHUNK_AT["ffn", s]
                load(first)
                load(first + 1)
                if s + 1 < NSB:
                    sp.wait_ge(y_taken, 4 * (s + 2))
                else:
                    sp.wait_ge(o_normed, R * (s + 1))
                sp.dma_start(p_rows, p[0, 0, s * SB:(s + 1) * SB, :].rearrange("(r p) n -> p r n", p=P)
                             ).then_inc(p_loaded, 16)
                last = CHUNK_AT["att", s + 1] + SLOTS if s + 1 < NSB else len(CHUNKS)
                for n in range(first + 2, last):
                    if n == first + FFN_CHUNKS:
                        load_gb2(s)
                    load(n)
                if last == first + FFN_CHUNKS:
                    load_gb2(s)
                for r in range(R):
                    g = row_tile(s, r)
                    sp.wait_ge(out_done, g + 1)
                    sp.dma_start(out[0, g * P:(g + 1) * P, :], rows[:, r, :]).then_inc(out_stored, 16)

            x_load(0)
            for i, src in enumerate((ln_emb_g, ln_emb_b, ln1_g[0], ln1_b[0])):
                sp.dma_start(ln_gb[:, i, :], src.rearrange("(k p) -> p k", p=P)).then_inc(ln_loaded, 16)
            for n in range(SLOTS):
                load(n)
            sp.dma_start(pos_i[:, :], positions[0].rearrange("(g p) -> p g", p=P)).then_inc(const_loaded, 16)
            for dst, src in ((s5c[:, 0, :], s5_lam_re[0].rearrange("g p -> (g p)")),
                             (s5c[:, 1, :], s5_lam_im[0].rearrange("g p -> (g p)")),
                             (d_col[:, :], s5_d[0]), (bglu_col[:, :], s5_b_glu[0]),
                             (rgc[:, 0, :], rg_conv_b[0]), (rgc[:, 1, :], rg_ba[0]),
                             (rgc[:, 2, :], rg_bx[0]), (rgc[:, 3, :], rg_lam[0])):
                sp.dma_start(dst, src.rearrange("(k p) -> p k", p=P)).then_inc(const_loaded, 16)
            for a in (0, 1):
                sp.dma_start(s5c[64 * a:64 * a + 64, 2, :],
                             s5_log_step[0].rearrange("(i a) -> a i", a=2)[a].partition_broadcast(64)
                             ).then_inc(const_loaded, 16)
            for k in range(RG_CONV):
                sp.dma_start(conv_w[:, :, k], rg_conv_w[0][k].rearrange("(c p) -> p c", p=P)
                             ).then_inc(const_loaded, 16)
            sp.dma_start(w_glu[:, :, :], s5_w_glu[0].rearrange("(k p) n -> p k n", p=P)).then_inc(const_loaded, 16)
            sp.dma_start(w_tail[:, :, :], w_in[0][:, C_KI:N_IN].rearrange("(k p) n -> p k n", p=P)
                         ).then_inc(const_loaded, 16)
            sp.wait_ge(blocks_zeroed, 4)
            for i, src in enumerate((s5_b_re, s5_b_im)):
                for a in (0, 1):
                    sp.dma_start(
                        blk_b[i][64 * a:64 * a + 64, :].rearrange("p (i a c) -> p i a c", i=NST, a=2)[:, :, a, :],
                        src[0].rearrange("(i a) p c -> a p i c", a=2)[a]).then_inc(blocks_loaded, 16)
            for i, src in enumerate((s5_c_re, s5_c_im)):
                for j in range(4):
                    for a in (0, 1):
                        q = 32 * j + 16 * a
                        sp.dma_start(
                            blk_c[i][q:q + 16, :].rearrange("c (t n) -> c t n", t=2)[:, :, 64 * a:64 * a + 64],
                            src[0].rearrange("(t j a) c p -> j a c t p", j=4, a=2)[j, a]).then_inc(blocks_loaded, 16)
            for i, src in enumerate((rg_wa, rg_wx)):
                for j in range(4):
                    sp.dma_start(w_gates[32 * j:32 * j + 32, i, :, 32 * j:32 * j + 32],
                                 src[0].rearrange("(c j) m n -> j m c n", j=4)[j]).then_inc(blocks_loaded, 16)

            spill_h(0)
            for n in range(SLOTS, 6):
                load(n)
            sp.wait_ge(dve_setup, SETUP_PHASES)
            sp.dma_start(phase_spill, phase[:, :, :, :]).then_inc(phase_spilled, 16)
            for n in range(6, 16):
                load(n)
            attend(0)
            for s in range(NSB):
                if s + 1 < NSB:
                    mix_in(s + 1)
                feed_forward(s)
                if s + 1 < NSB:
                    attend(s + 1)
            sp.wait_ge(out_stored, 16 * SEQ // P)
            sp.wait_ge(h_spilled, 16 * NSB)

        CONSTS = 1 + 8 + 2 + RG_CONV + 2
        BLOCKS = 4 + 16 + 8

        @block.gpsimd
        def _(pool):
            def norm(call):
                n = NORM[call]
                pool.wait_ge(aggr_done, R * (n + 1))
                pool.tensor_scalar(var_eps[:, :], mv[:, :, 1], EPS, None, ALU.add).then_inc(rstd_done, 1)
                pool.wait_ge(rstd_done, 2 * n + 1)
                pool.tensor_tensor(rstd[:, :], var_eps[:, :], neg_half[:, :], ALU.pow).then_inc(rstd_done, 1)

            def rope(s, j):
                job = 3 * R * s + j
                grp, r = divmod(j, R)
                pool.wait_ge(proj_taken, job + 1)
                if grp:
                    pool.wait_ge(turned, T_AT["mix", s] + turned_banks(j - R)[-1] + 1)
                dst = roped[r]
                if grp == 0:
                    pool.tensor_tensor(dst.rearrange("p (j g d) -> p g j d", j=4, g=2),
                                       rope_a.rearrange("p (g j d) -> p g j d", g=2, j=4),
                                       rope_b.rearrange("p (g j d) -> p g j d", g=2, j=4),
                                       ALU.add).then_inc(rope_done, 1)
                elif grp == 1:
                    pool.tensor_tensor(dst[:, 0:192], rope_a[:, 0:192], rope_b[:, 0:192], ALU.add)
                    pool.tensor_tensor(dst[:, 192:256], rope_a[:, 128:192], rope_b[:, 128:192],
                                       ALU.add).then_inc(rope_done, 1)
                else:
                    pool.tensor_tensor(dst, rope_a, rope_b, ALU.add).then_inc(rope_done, 1)

            splits = [0]

            def split_until(n):
                for m in range(splits[0], splits_until(n)):
                    pool.wait_ge(split_high, m + 1)
                    high, low = pairs[:, m % SLOTS, 0, :], pairs[:, m % SLOTS, 1, :]
                    pool.tensor_tensor(low, ring[:, SPLITS[m] % SLOTS, :], high.bitcast(f32), ALU.subtract
                                       ).then_inc(split_low, 1)
                    splits[0] = m + 1

            def split_h1(s):
                pool.wait_ge(turned_taken, T_AT["one", s] + KT)
                for k in range(KT):
                    pool.tensor_copy(h1_pair[0][:, k, :], h1T[:, k, :]).then_inc(h1_split, 1)
                for k in range(KT):
                    pool.wait_ge(h1_split, 2 * KT * s + k + 1)
                    pool.tensor_tensor(h1_pair[1][:, k, :], h1T[:, k, :], h1_pair[0][:, k, :].bitcast(f32),
                                       ALU.subtract).then_inc(h1_split, 1)

            def gelu_arg(src, dst, done, at):
                pool.tensor_tensor(dst, src, src, ALU.mult).then_inc(done, 1)
                pool.wait_ge(done, at + 1)
                pool.tensor_scalar(dst, dst, GELU_C, 1.0, ALU.mult, ALU.add).then_inc(done, 1)
                pool.wait_ge(done, at + 2)
                pool.tensor_tensor(dst, dst, src, ALU.mult).then_inc(done, 1)

            def s5_rotate(n):
                m, w = s5_m, s5_w[n % 2]
                pool.wait_ge(s5_mixed, 2 * (n + 1))
                if n >= 2:
                    pool.wait_ge(s5_scanned, 4 * (n - 2) + 2)
                pool.tensor_tensor(w[:, 0, :], m[:, 0, 0, :], m[:, 0, 1, :], ALU.add)
                pool.tensor_tensor(w[:, 1, :], m[:, 1, 0, :], m[:, 1, 1, :], ALU.subtract).then_inc(s5_rotated, 1)

            def s5_finish(n):
                i = n % NST
                xs = s5_x[n % 2]
                pool.wait_ge(s5_scanned, 4 * (n + 1))
                if n >= 2:
                    pool.wait_ge(y_ready, n - 1)
                pool.tensor_tensor(xs[:, 0, :], s5_n[:, 0, 0, :], s5_n[:, 0, 1, :], ALU.subtract)
                pool.tensor_tensor(xs[:, 1, :], s5_n[:, 1, 0, :], s5_n[:, 1, 1, :], ALU.add).then_inc(s5_state, 1)
                pool.wait_ge(s5_state, 2 * n + 1)
                pool.tensor_copy(s5_carry[:, i, :], xs[:, :, TW - 1]).then_inc(s5_state, 1)

            def mix_in(s):
                pool.wait_ge(feat_taken, 10 * s + 6)
                gelu_arg(gate_t, gelu_t, rg_pool, 7 * s)
                pool.wait_ge(feat_taken, 10 * s + 10)
                for c in (0, 1):
                    pool.tensor_scalar(ra_t[:, c, :], ra_t[:, c, :], 1.0, rgc[:, 4, c:c + 1],
                                       ALU.add, ALU.mult).then_inc(rg_pool, 1)
                pool.wait_ge(rg_act, 4 * s + 3)
                pool.wait_ge(rg_dve, 6 * s + 2)
                pool.tensor_tensor(conv_t, a_t, a_t, ALU.mult).then_inc(rg_pool, 1)
                pool.wait_ge(rg_act, 4 * s + 4)
                pool.tensor_tensor(ib_t, ib_t, conv_t, ALU.mult).then_inc(rg_pool, 1)
                for t, slot in enumerate(SLOT_LIST):
                    n = s5_step_of(t)
                    if n is not None and n < STEPS:
                        s5_rotate(STEPS * s + n)
                    if n is not None and 1 <= n <= STEPS:
                        s5_finish(STEPS * s + n - 1)
                    j = rope_job(slot)
                    if j is not None:
                        rope(s, j)
                pool.wait_ge(y_taken, 4 * (s + 1))
                pool.wait_ge(rg_dve, 6 * s + 3)
                gelu_arg(u_t, gelu_t, gl_pool, 4 * s)
                pool.wait_ge(gl_dve, 2 * (s + 1))
                pool.tensor_scalar(mixT[:, 0:2, :], u_t, 0.25, None, ALU.mult).then_inc(gl_pool, 1)
                if s:
                    pool.wait_ge(proj_ready, 3 * R * (s + 1))
                    pool.wait_ge(h_spilled, 16 * (s + 1))
                    split_h1(s - 1)
                done = idx_before(s)
                for r in range(R):
                    g = row_tile(s, r)
                    w, at = width(g), score_at(s, r)
                    if selects(g):
                        done += logit_jobs_of(g)
                        pool.wait_ge(idx_summed, done)
                        pool.affine_select(out=scores[:, at + w - P:at + w], in_=scores[:, at + w - P:at + w],
                                           compare_op=ALU.is_ge, fill=NEG, base=0, pattern=[[-1, P]],
                                           channel_multiplier=1).then_inc(causal_done, 1)
                    else:
                        pool.wait_ge(gl_pool, 4 * (s + 1))
                        pool.wait_ge(rg_dve, 6 * (s + 1))
                        pool.memset(scores[:, at:at + w], 0.0).then_inc(causal_done, 1)
                        pool.wait_ge(causal_done, 2 * g + 1)
                        pool.affine_select(out=scores[:, at + w - P:at + w], in_=scores[:, at + w - P:at + w],
                                           compare_op=ALU.is_ge, fill=-BIG, base=0, pattern=[[-1, P]],
                                           channel_multiplier=1).then_inc(causal_done, 1)
                if s:
                    split_until(CHUNK_AT["ffn", s - 1] + 1)

            def attend(s):
                c0 = CHUNK_AT["att", s]
                for k in range(4):
                    pool.wait_ge(mix_high, 8 * s + k + 1)
                    pool.tensor_tensor(mix_pair[1][k], mixT[:, k, :], mix_pair[0][k].bitcast(f32),
                                       ALU.subtract).then_inc(mix_low, 1)
                split_until(c0 + 1)
                pool.wait_ge(mix_low, 8 * s + 4)
                for r in range(R):
                    g = row_tile(s, r)
                    pool.wait_ge(inv_done, g + 1)
                    if g:
                        pool.wait_ge(turned, t_out(g - 1) + 1)
                    pool.tensor_tensor(inv_diag, ident[:, :].unsqueeze(1).to_broadcast([P, HEADS, P]),
                                       inv_sum[:, g % 2, :].unsqueeze(2).to_broadcast([P, HEADS, P]),
                                       ALU.mult).then_inc(diag_done, 1)
                    pool.wait_ge(mix_high, 8 * s + 4 + r + 1)
                    pool.tensor_tensor(mixT_parts[:, 0:4, r * P:(r + 1) * P],
                                       o_turned[g % 2].rearrange("p (j q) -> p j q", j=4),
                                       mixT_parts[:, 4:8, r * P:(r + 1) * P].bitcast(f32),
                                       ALU.subtract).then_inc(mix_low, 1)
                if s + 1 < NSB:
                    split_until(c0 + 7)
                    norm(("emb", s + 1))
                split_until(c0 + 9)
                norm(("one", s))

            def feed_forward(s):
                c0 = CHUNK_AT["ffn", s]
                if s + 1 == NSB:
                    split_until(c0 + 1)
                    split_h1(s)
                for c in (0, 1):
                    split_until(c0 + (11 if c else 6))
                    for r in range(R):
                        n = 2 * R * s + R * c + r
                        pool.wait_ge(pp_taken, n + 1)
                        pool.wait_ge(pg_taken, n + 1)
                        pool.tensor_scalar(evac_b[n % 2], evac_b[n % 2], 1.0, None, ALU.add).then_inc(ple_half, 1)
                        pool.wait_ge(ple_half, n + 1)
                        pool.tensor_tensor(rows[:, r, c * 512:(c + 1) * 512], evac_b[n % 2], half_pp[r],
                                           ALU.mult).then_inc(ple_done, 1)
                c0 += 10
                for kind, i in FFN_STEPS:
                    if kind == "up":
                        f = NF * s + i
                        silu = tanh_b[f % 2]
                        split_until(c0 + 3)
                        pool.wait_ge(act_one, f + 1)
                        pool.tensor_tensor(silu, silu, gate_b[f % 2], ALU.mult).then_inc(act_half, 1)
                        pool.wait_ge(up_taken, 3 * (f + 1))
                        pool.wait_ge(act_half, 2 * f + 1)
                        pool.tensor_tensor(silu, silu, up_b[f % 2], ALU.mult).then_inc(act_half, 1)
                        split_until(c0 + 4)
                        pool.wait_ge(act_high, f + 1)
                        pool.tensor_tensor(act_pair[1][i % ACTS], silu, act_pair[0][i % ACTS].bitcast(f32),
                                           ALU.subtract).then_inc(act_done, 1)
                        c0 += 2
                        continue
                    for c in (0, 1):
                        c0 += PARTS[i][1] // 2
                        split_until(c0 + 1)
                        for r in range(R):
                            n = DOWN_JOBS * s + 2 * R * i + R * c + r
                            pool.wait_ge(down_taken, n + 1)
                            if i:
                                pool.wait_ge(down_added, n - 2 * R + 1)
                            dst = rows[:, r, c * 512:(c + 1) * 512]
                            pool.tensor_tensor(dst, dst, down_b[n % 4], ALU.add).then_inc(down_added, 1)
                norm(("two", s))
                pool.wait_ge(gb2_loaded, 32 * (s + 1))
                for r in range(R):
                    g = row_tile(s, r)
                    pool.wait_ge(normed, R * NORM["two", s] + r + 1)
                    pool.tensor_tensor(rows[:, r, :], rows[:, r, :], gb2[:, 0, :], ALU.mult).then_inc(out_scaled, 1)
                    pool.wait_ge(out_scaled, g + 1)
                    pool.tensor_tensor(rows[:, r, :], rows[:, r, :], gb2[:, 1, :], ALU.add).then_inc(out_done, 1)

            for i in (0, 1):
                pool.memset(blk_b[i], 0.0).then_inc(blocks_zeroed, 1)
            pool.memset(setup[:, 1024:1536], 0.0).then_inc(blocks_zeroed, 1)
            pool.memset(w_gates[:, :, :, :], 0.0).then_inc(blocks_zeroed, 1)
            pool.memset(ident[:, :], 0.0).then_inc(pool_setup, 1)
            pool.wait_ge(pool_setup, 1)
            pool.affine_select(out=ident[:, :], in_=ident[:, :], compare_op=ALU.not_equal, fill=1.0,
                               base=0, pattern=[[-1, P]], channel_multiplier=1).then_inc(pool_setup, 1)
            pool.wait_ge(pool_setup, 2)
            pool.tensor_scalar(alpha_i[:, :], ident[:, :], ALPHA, None, ALU.mult)
            pool.memset(neg_half[:, :], -0.5)
            pool.memset(ones[:, :], 1.0)
            pool.memset(s5_carry[:, :, :], 0.0)
            pool.memset(halo[:, :, :], 0.0)
            pool.memset(rg_carry[:, :], 0.0)
            for i in range(32):
                pool.memset(inv_f[:, i:i + 1], float(np.float32(10000.0) ** np.float32(-2.0 * i / HD)))
            pool.memset(rstd[:, :], 0.0).then_inc(pool_setup, 1)

            norm(("emb", 0))
            mix_in(0)
            attend(0)
            for s in range(NSB):
                if s + 1 < NSB:
                    mix_in(s + 1)
                feed_forward(s)
                if s + 1 < NSB:
                    attend(s + 1)

        @block.scalar
        def _(scalar):
            def take(t, dst, src, **kw):
                scalar.wait_ge(turned, t + 1)
                scalar.activation(dst, src, **kw).then_inc(turned_taken, 1)

            splits = [0]

            def split_until(n):
                for m in range(splits[0], splits_until(n)):
                    c = SPLITS[m]
                    scalar.wait_ge(chunk_loaded[c % SLOTS], 16 * (c // SLOTS + 1))
                    if m >= SLOTS:
                        scalar.wait_ge(chunk_used, SPLITS[m - SLOTS] + 2)
                    scalar.activation(pairs[:, m % SLOTS, 0, :], ring[:, c % SLOTS, :], ACT.Copy
                                      ).then_inc(split_high, 1)
                    splits[0] = m + 1

            def norm_turned(t0, dst, g_row):
                for k in range(KT):
                    t = t0 + k
                    take(t, dst[:, k, :], tbank[t % 2][:, :], func=ACT.Identity,
                         scale=ln_gb[:, g_row, k:k + 1], bias=ln_gb[:, g_row + 1, k:k + 1])

            def features(s):
                for m in range(6):
                    n = 10 * s + m
                    src = bank[4 + n % 2][:, :]
                    if m == 0:
                        scalar.activation(xr_t[:, :, 0:3], halo[:, :, :], ACT.Copy).then_inc(halo_done, 1)
                    scalar.wait_ge(feat_ready, n + 1)
                    dst = (xr_t[:, 0, 3:515], xr_t[:, 1, 3:515], u_t[:, 0, :], u_t[:, 1, :],
                           gate_t[:, 0, :], gate_t[:, 1, :])[m]
                    scalar.activation(dst, src, ACT.Copy).then_inc(feat_taken, 1)
                    if m == 1:
                        scalar.wait_ge(feat_taken, n + 1)
                        scalar.wait_ge(halo_done, 2 * s + 1)
                        scalar.activation(halo[:, :, :], xr_t[:, :, 512:515], ACT.Copy).then_inc(halo_done, 1)

            def mix_in(s):
                t0 = T_AT["mix", s]
                for m in range(4):
                    n = 10 * s + 6 + m
                    kind, c = divmod(m, 2)
                    scalar.wait_ge(feat_ready, n + 1)
                    scalar.activation((ra_t, ib_t)[kind][:, c, :], bank[4 + n % 2][:, :], ACT.Tanh, scale=0.5,
                                      bias=rgc[:, 5 + kind, c:c + 1]).then_inc(feat_taken, 1)
                scalar.wait_ge(rg_pool, 7 * s + 3)
                scalar.activation(gelu_t, gelu_t, ACT.Tanh, scale=GELU_K).then_inc(rg_act, 1)
                scalar.wait_ge(rg_pool, 7 * s + 5)
                scalar.wait_ge(conv_done, 8 * (s + 1))
                scalar.wait_ge(halo_done, 2 * s + 2)
                scalar.activation(a_t, ra_t, ACT.Exp).then_inc(rg_act, 1)
                scalar.wait_ge(rg_act, 4 * s + 2)
                scalar.activation(ra_t, ra_t, ACT.Tanh, scale=-1.0).then_inc(rg_act, 1)
                scalar.wait_ge(rg_dve, 6 * s + 3)
                scalar.activation(conv_t, conv_t, ACT.Sqrt, scale=0.25).then_inc(rg_act, 1)
                for slot in SLOT_LIST:
                    j = transposed_in(slot)
                    if j is None:
                        continue
                    grp, r = divmod(j, R)
                    g = row_tile(s, r)
                    for i, b in enumerate(turned_banks(j)):
                        t = t0 + b
                        src = tbank[t % 2][:, :].rearrange("p (j q) -> p j q", j=4)
                        if grp == 0:
                            take(t, qT[:, :, r * P:(r + 1) * P], src, func=ACT.Copy, scale=HD ** -0.5)
                            continue
                        scalar.wait_ge(turned, t + 1)
                        if grp == 1:
                            scalar.activation(keysT[:, g * P:(g + 1) * P], src[:, 0, :], ACT.Copy)
                            dst, src = idx_keys[:, 0, g * P:(g + 1) * P], src[:, 1, :]
                            scalar.activation(dst, src, ACT.Copy).then_inc(turned_high, 1)
                            continue
                        scalar.activation(idx_qT[0:HD, 4 * i:4 * i + 4, r * P:(r + 1) * P], src[0:HD, :, :], ACT.Copy)
                        for at, h, heads in lower_heads(i):
                            ins = scalar.activation(idx_qT[HD:P, h:h + heads, r * P:(r + 1) * P],
                                                    src[HD:P, at:at + heads, :], ACT.Copy)
                        ins.then_inc(turned_high, 1)
                scalar.wait_ge(gl_pool, 4 * s + 3)
                scalar.activation(gelu_t, gelu_t, ACT.Tanh, scale=GELU_K).then_inc(gl_act, 1)
                for c in (0, 1):
                    scalar.wait_ge(glu_ready, 2 * s + c + 1)
                    scalar.activation(gelu_t[:, c, :], bank[4 + c][:, :], ACT.Tanh, scale=0.25,
                                      bias=s5c[:, 20 + c, 0:1]).then_inc(glu_taken, 1)
                n = idx_before(s)
                for r, h, a, w in idx_jobs(s):
                    scalar.wait_ge(idx_ready, n + 1)
                    if n >= 3:
                        scalar.wait_ge(idx_summed, n - 2)
                    scalar.activation(relu_buf[n % 3][:, 0:w], bank[n % 4][:, 0:w], ACT.Relu
                                      ).then_inc(idx_taken, 1)
                    n += 1
                if s:
                    split_until(CHUNK_AT["ffn", s - 1] + 1)

            def attend(s):
                if s:
                    scalar.wait_ge(act_done, NF * s)

                def scale_turned(g):
                    t = t_out(g)
                    if g % R >= 2:
                        scalar.wait_ge(o_normed, g - 1)
                    take(t, o_scale[g % 2], tbank[t % 2][:, :], func=ACT.Copy)

                def high_part(g):
                    r = g % R
                    scalar.wait_ge(o_normed, g + 1)
                    scalar.activation(mixT_parts[:, 4:8, r * P:(r + 1) * P],
                                      o_turned[g % 2].rearrange("p (j q) -> p j q", j=4), ACT.Copy
                                      ).then_inc(mix_high, 1)

                c0 = CHUNK_AT["att", s]
                scalar.wait_ge(rg_dve, 6 * (s + 1))
                scalar.wait_ge(gl_pool, 4 * (s + 1))
                scalar.wait_ge(phase_spilled, 16)
                for k in range(4):
                    scalar.activation(mix_pair[0][k], mixT[:, k, :], ACT.Copy).then_inc(mix_high, 1)
                split_until(c0 + 1)
                for r in range(R):
                    g = row_tile(s, r)
                    w = width(g)
                    for h in range(HEADS):
                        n = HEADS * g + h
                        scalar.wait_ge(max_ready, n + 1)
                        if h == 0 and g >= 2:
                            scalar.wait_ge(inv_done, g - 1)
                        scalar.activation(prob[n % 2][:, 0:w], prob[n % 2][:, 0:w], ACT.Exp,
                                          bias=neg_max[:, n % 2:n % 2 + 1],
                                          accum_out=row_sum[:, g % 2, h:h + 1]).then_inc(exp_done, 1)
                        t = t_attn(g, h)
                        if n >= 2:
                            scalar.wait_ge(pv_done, n - 1)
                        for a, pw in pieces(w):
                            take(t, probT[n % 2][:, a:a + pw], tbank[t % 2][:, 0:pw], func=ACT.Copy)
                            t += 1
                        if h == 0 and r:
                            scale_turned(g - 1)
                        if h == 2 and r:
                            high_part(g - 1)
                scale_turned(row_tile(s, R - 1))
                high_part(row_tile(s, R - 1))
                for c in (0, 1):
                    split_until(c0 + (9 if c else 7))
                    for r in range(R):
                        n = 2 * R * s + R * c + r
                        scalar.wait_ge(mixed_ready, n + 1)
                        if s and c == 0:
                            scalar.wait_ge(out_stored, 16 * R * s)
                        scalar.activation(rows[:, r, c * 512:(c + 1) * 512], bank[r][:, :], ACT.Copy
                                          ).then_inc(mixed_taken, 1)
                if s + 1 == NSB:
                    split_until(CHUNK_AT["ffn", s] + 1)

            def feed_forward(s):
                for k in range(D_PLE // P):
                    t = T_AT["ffn", s] + k
                    take(t, pT[:, k, :], tbank[t % 2][:, :], func=ACT.Copy)
                c0 = CHUNK_AT["ffn", s]
                for c in (0, 1):
                    split_until(c0 + (7 if c else 2))
                    for r in range(R):
                        n = 2 * R * s + R * c + r
                        scalar.wait_ge(pp_ready, n + 1)
                        if c:
                            scalar.wait_ge(ple_done, n - R + 1)
                        scalar.activation(half_pp[r], bank[4 + n % 2][:, :], ACT.Copy, scale=0.5
                                          ).then_inc(pp_taken, 1)
                    split_until(c0 + (11 if c else 6))
                    for r in range(R):
                        n = 2 * R * s + R * c + r
                        scalar.wait_ge(pg_ready, n + 1)
                        if n >= 2:
                            scalar.wait_ge(ple_done, n - 1)
                        scalar.activation(evac_b[n % 2], bank[r][:, :], ACT.Tanh, scale=0.5).then_inc(pg_taken, 1)
                scalar.wait_ge(ple_done, 2 * R * (s + 1))
                if s + 1 < NSB:
                    scalar.wait_ge(y_taken, 4 * (s + 2))
                    scalar.wait_ge(idx_summed, idx_before(s + 2))
                c0 += 10
                for kind, i in FFN_STEPS:
                    if kind == "up":
                        f = NF * s + i
                        gate, up = bank[4 + 2 * (f % 2)], bank[5 + 2 * (f % 2)]
                        split_until(c0 + 3)
                        scalar.wait_ge(up_ready, 2 * f + 1)
                        if f >= 2:
                            scalar.wait_ge(act_done, f - 1)
                        scalar.activation(tanh_b[f % 2], gate[:, :], ACT.Tanh, scale=0.5).then_inc(up_taken, 1)
                        scalar.activation(gate_b[f % 2], gate[:, :], ACT.Copy).then_inc(up_taken, 1)
                        scalar.wait_ge(up_taken, 3 * f + 1)
                        scalar.activation(tanh_b[f % 2], tanh_b[f % 2], ACT.Copy, bias=1.0).then_inc(act_one, 1)
                        scalar.wait_ge(up_ready, 2 * f + 2)
                        scalar.activation(up_b[f % 2], up[:, :], ACT.Copy, scale=0.5).then_inc(up_taken, 1)
                        split_until(c0 + 4)
                        scalar.wait_ge(act_half, 2 * f + 2)
                        if i >= ACTS:
                            scalar.wait_ge(down_ready, DOWN_JOBS * s + 2 * R * (part_of(i - ACTS) + 1))
                        scalar.activation(act_pair[0][i % ACTS], tanh_b[f % 2], ACT.Copy).then_inc(act_high, 1)
                        c0 += 2
                        continue
                    for c in (0, 1):
                        c0 += PARTS[i][1] // 2
                        split_until(c0 + 1)
                        for r in range(R):
                            n = DOWN_JOBS * s + 2 * R * i + R * c + r
                            scalar.wait_ge(down_ready, n + 1)
                            if n >= 4:
                                scalar.wait_ge(down_added, n - 3)
                            scalar.activation(down_b[n % 4], bank[r][:, :], ACT.Copy).then_inc(down_taken, 1)

            scalar.wait_ge(ln_loaded, 64)
            norm_turned(T_AT["emb", 0], hT, 0)
            scalar.wait_ge(const_loaded, 16 * CONSTS)
            scalar.activation(s5c[:, 3, :], s5c[:, 2, :], ACT.Exp).then_inc(act_setup, 1)
            scalar.activation(rgc[:, 7, :], rgc[:, 3, :], ACT.Abs).then_inc(act_setup, 1)
            scalar.wait_ge(act_setup, 2)
            scalar.activation(rgc[:, 8, :], rgc[:, 7, :], ACT.Exp, scale=-1.0).then_inc(act_setup, 1)
            scalar.wait_ge(dve_setup, 1)
            scalar.activation(s5c[:, 5, :], s5c[:, 4, :], ACT.Exp).then_inc(act_setup, 1)
            scalar.wait_ge(dve_setup, SETUP_ANGLES)
            scalar.activation(s5c[:, 8, :], s5c[:, 6, :], ACT.Sin)
            scalar.activation(s5c[:, 9, :], s5c[:, 7, :], ACT.Sin)
            scalar.activation(sin_t[:, :, 1, :], tmp_a[:, 0:512].rearrange("p (g f) -> p g f", g=16), ACT.Sin)
            scalar.activation(cos_t[:, :, :], tmp_b[:, 0:512].rearrange("p (g f) -> p g f", g=16), ACT.Sin)
            scalar.activation(sin_t[:, :, 0, :], tmp_a[:, 0:512].rearrange("p (g f) -> p g f", g=16), ACT.Sin,
                              scale=-1.0).then_inc(act_setup, 1)
            features(0)
            t = T_AT["setup", 0]
            take(t, bT[:, :, :, :], tbank[0][:, :].rearrange("p (m t q) -> p m t q", m=2, t=2), func=ACT.Copy)
            scalar.wait_ge(turned, t + 2)
            scalar.activation(cT[:, 0, :, :], tbank[1][:, 0:256].rearrange("p (i c) -> p i c", c=32), ACT.Copy)
            scalar.activation(cT[:, 1, :, :], tbank[1][:, 256:512].rearrange("p (i c) -> p i c", c=32), ACT.Copy,
                              scale=-1.0).then_inc(turned_taken, 1)

            mix_in(0)
            attend(0)
            for s in range(NSB):
                if s + 1 < NSB:
                    norm_turned(T_AT["emb", s + 1], hT, 0)
                    features(s + 1)
                norm_turned(T_AT["one", s], h1T, 2)
                if s + 1 < NSB:
                    mix_in(s + 1)
                feed_forward(s)
                if s + 1 < NSB:
                    attend(s + 1)

        @block.vector
        def _(dve):
            setup_n = [0]

            def link(ins):
                setup_n[0] += 1
                ins.then_inc(dve_setup, 1)
                dve.wait_ge(dve_setup, setup_n[0])

            def norm(call, ready, tiles=rows):
                n = NORM[call]
                for half in (0, 1):
                    for r in range(R):
                        ready(half, r)
                        ins = dve.bn_stats(stats[:, r, half, :], tiles[:, r, half * 512:(half + 1) * 512])
                        if half:
                            ins.then_inc(stats_done, 1)
                for r in range(R):
                    dve.wait_ge(stats_done, R * n + r + 1)
                    dve.bn_aggr(mv[:, r, :], stats[:, r, :, :].rearrange("p a b -> p (a b)")).then_inc(aggr_done, 1)
                dve.wait_ge(rstd_done, 2 * (n + 1))
                for r in range(R):
                    dve.tensor_scalar(tiles[:, r, :], tiles[:, r, :], mv[:, r, 0:1], rstd[:, r:r + 1],
                                      ALU.subtract, ALU.mult).then_inc(normed, 1)

            def rope(s, j):
                job = 3 * R * s + j
                grp, r = divmod(j, R)
                g = row_tile(s, r)
                src = bank[r]
                dve.wait_ge(proj_ready, job + 1)
                if j:
                    dve.wait_ge(rope_done, job)

                def products(a, heads, at):
                    view = src[:, a:a + heads * HD].rearrange("p (h c f) -> p h c f", h=heads, c=2)
                    to = [t[:, at:at + heads * HD].rearrange("p (h c f) -> p h c f", h=heads, c=2)
                          for t in (rope_a, rope_b)]
                    cs = cos_t[:, g, :].unsqueeze(1).unsqueeze(1).to_broadcast([P, heads, 2, 32])
                    sn = sin_t[:, g, :, :].unsqueeze(1).to_broadcast([P, heads, 2, 32])
                    dve.tensor_tensor(to[0], view, cs, ALU.mult)
                    return dve.tensor_tensor(to[1], view[:, :, ::-1, :], sn, ALU.mult)

                if grp != 1:
                    products(0, HEADS, 0).then_inc(proj_taken, 1)
                    return
                products(0, KVH, 0)
                products(256, 1, P)
                dve.tensor_copy(vals[:, g, :], src[:, P:2 * P])
                dve.tensor_scalar(w_idx[:, r, :], src[:, 320:328], (HEADS * HD) ** -0.5, None,
                                  ALU.mult).then_inc(proj_taken, 1)

            def s5_mix(n):
                i = n % NST
                dve.wait_ge(bu_ready, n + 1)
                if n:
                    dve.wait_ge(s5_rotated, n)
                bu = bank[4][:, :].rearrange("p (c t) -> p c t", c=2)
                dve.tensor_tensor(s5_m[:, 0, :, :], bu, phase[:, i, :, :], ALU.mult).then_inc(s5_mixed, 1)
                dve.tensor_tensor(s5_m[:, 1, :, :], bu[:, ::-1, :], phase[:, i, :, :], ALU.mult
                                  ).then_inc(s5_mixed, 1)

            def s5_scan(n):
                i = n % NST
                mag = s5c[:, 5, i:i + 1].to_broadcast([P, TW])
                dve.wait_ge(s5_rotated, n + 1)
                if n >= NST:
                    dve.wait_ge(s5_state, 2 * (n - NST + 1))
                if n:
                    dve.wait_ge(s5_scanned, 4 * n)
                for c in (0, 1):
                    dve.tensor_tensor_scan(s5_z[:, c, :], mag, s5_w[n % 2][:, c, :], s5_carry[:, i, c:c + 1],
                                           ALU.mult, ALU.add).then_inc(s5_scanned, 1)
                dve.wait_ge(s5_scanned, 4 * n + 2)
                if n:
                    dve.wait_ge(s5_state, 2 * n - 1)
                dve.tensor_tensor(s5_n[:, 0, :, :], s5_z[:, :, :], phase[:, i, :, :], ALU.mult
                                  ).then_inc(s5_scanned, 1)
                dve.tensor_tensor(s5_n[:, 1, :, :], s5_z[:, ::-1, :], phase[:, i, :, :], ALU.mult
                                  ).then_inc(s5_scanned, 1)

            def y_take(s, sub):
                n = 4 * s + 2 * sub
                dve.wait_ge(y_ready, STEPS * s + NST * (sub + 1))
                for c in (0, 1):
                    part = u_t[:, c, sub * TW:(sub + 1) * TW]
                    dve.scalar_tensor_tensor(part, part, d_col[:, c:c + 1], bank[5][:, c * TW:(c + 1) * TW],
                                             ALU.mult, ALU.add).then_inc(y_taken, 1)

            def low_parts(s, j):
                if j is None or j < R:
                    return
                r = j % R
                for i, b in enumerate(turned_banks(j)):
                    t = T_AT["mix", s] + b
                    src = tbank[t % 2][:, :].rearrange("p (j q) -> p j q", j=4)
                    dve.wait_ge(turned_high, 3 * R * s + b - R + 1)
                    if j < 2 * R:
                        cols = slice(row_tile(s, r) * P, (row_tile(s, r) + 1) * P)
                        ins = dve.tensor_tensor(idx_keys[:, 1, cols], src[:, 1, :],
                                                idx_keys[:, 0, cols].bitcast(f32), ALU.subtract)
                    else:
                        for at, h, heads in lower_heads(i):
                            dst = idx_qT[HD:P, h:h + heads, r * P:(r + 1) * P]
                            ins = dve.tensor_tensor(dst, src[HD:P, at:at + heads, :], dst.bitcast(f32), ALU.subtract)
                    ins.then_inc(turned_taken, 1)

            def mix_in(s):
                n = 8 * s
                dve.wait_ge(feat_taken, 10 * s + 2)
                dve.wait_ge(halo_done, 2 * s + 1)
                for k in range(RG_CONV):
                    for c in (0, 1):
                        src = xr_t[:, c, k:k + 512]
                        if k == 0:
                            ins = dve.tensor_scalar(conv_t[:, c, :], src, conv_w[:, c, 0:1], rgc[:, 0, c:c + 1],
                                                    ALU.mult, ALU.add)
                        else:
                            dve.wait_ge(conv_done, n - 1)
                            ins = dve.scalar_tensor_tensor(conv_t[:, c, :], src, conv_w[:, c, k:k + 1],
                                                           conv_t[:, c, :], ALU.mult, ALU.add)
                        ins.then_inc(conv_done, 1)
                        n += 1
                dve.wait_ge(feat_taken, 10 * (s + 1))
                dve.scalar_tensor_tensor(ib_t, ib_t, 1.0, conv_t, ALU.add, ALU.mult).then_inc(rg_dve, 1)
                dve.wait_ge(rg_act, 4 * s + 1)
                dve.scalar_tensor_tensor(gate_t, gelu_t, 1.0, gate_t, ALU.add, ALU.mult).then_inc(rg_dve, 1)
                dve.wait_ge(rg_pool, 7 * s + 6)
                dve.wait_ge(rg_act, 4 * s + 3)
                dve.scalar_tensor_tensor(conv_t, conv_t, 1.0, ra_t, ALU.add, ALU.mult).then_inc(rg_dve, 1)
                dve.wait_ge(rg_pool, 7 * (s + 1))
                dve.wait_ge(rg_dve, 6 * s + 3)
                for c in (0, 1):
                    dve.tensor_tensor_scan(ra_t[:, c, :], a_t[:, c, :], ib_t[:, c, :], rg_carry[:, c:c + 1],
                                           ALU.mult, ALU.add).then_inc(rg_dve, 1)
                dve.wait_ge(rg_dve, 6 * s + 5)
                dve.tensor_copy(rg_carry[:, :], ra_t[:, :, 511])
                dve.scalar_tensor_tensor(mixT[:, 2:4, :], ra_t, 0.5, gate_t, ALU.mult, ALU.mult
                                         ).then_inc(rg_dve, 1)
                if s:
                    dve.wait_ge(phase_loaded, 16 * s)
                for t, slot in enumerate(SLOT_LIST):
                    n = s5_step_of(t)
                    if n is not None and n < STEPS:
                        s5_mix(STEPS * s + n)
                    if n is not None and 1 <= n <= STEPS:
                        s5_scan(STEPS * s + n - 1)
                    if n == NST + 1:
                        y_take(s, 0)
                    if n == STEPS + 1:
                        y_take(s, 1)
                    j = rope_job(slot)
                    if j is not None:
                        rope(s, j)
                    if t >= 2:
                        low_parts(s, transposed_in(SLOT_LIST[t - 2]))
                for slot in SLOT_LIST[-2:]:
                    low_parts(s, transposed_in(slot))
                dve.wait_ge(gl_act, s + 1)
                dve.scalar_tensor_tensor(u_t, gelu_t, 1.0, u_t, ALU.add, ALU.mult).then_inc(gl_dve, 1)
                dve.wait_ge(glu_taken, 2 * (s + 1))
                dve.wait_ge(gl_dve, 2 * s + 1)
                dve.scalar_tensor_tensor(u_t, gelu_t, 1.0, u_t, ALU.add, ALU.mult).then_inc(gl_dve, 1)
                n = idx_before(s)
                if idx_jobs(s):
                    dve.wait_ge(gl_pool, 4 * (s + 1))
                for r, h, a, w in idx_jobs(s):
                    part = scores[:, score_at(s, r) + a:score_at(s, r) + a + w]
                    src = relu_buf[n % 3][:, 0:w]
                    wh = w_idx[:, r, h:h + 1]
                    dve.wait_ge(idx_taken, n + 1)
                    if h == 0:
                        if n == idx_before(s):
                            dve.wait_ge(rg_dve, 6 * (s + 1))
                        dve.tensor_scalar(part, src, wh, None, ALU.mult).then_inc(idx_summed, 1)
                    else:
                        dve.wait_ge(idx_summed, n + 1 - len(pieces(width(row_tile(s, r)))))
                        dve.scalar_tensor_tensor(part, src, wh, part, ALU.mult, ALU.add).then_inc(idx_summed, 1)
                    n += 1
                for pair in ((0, 1), (2, 3)):
                    if not selects(row_tile(s, pair[0])):
                        continue
                    sel = [scores[:, score_at(s, r):score_at(s, r) + width(row_tile(s, r))] for r in pair]
                    edge = causal_before(row_tile(s, pair[1]) + 1)
                    dve.wait_ge(causal_done, edge)
                    per = 4
                    with dve.Fori(0, TOPK // 8 // per):
                        for u in range(per):
                            for i in (0, 1):
                                if u:
                                    dve.wait_ge(topk_step, 4 * (u - 1) + 3 + i)
                                dve.max(top8[:, i, :], sel[i]).then_inc(topk_step, 1)
                            for i in (0, 1):
                                dve.wait_ge(topk_step, 4 * u + 1 + i)
                                dve.match_replace(sel[i], top8[:, i, :], sel[i], MARK).then_inc(topk_step, 1)
                        dve.wait_ge(topk_step, 4 * per)
                        dve.sem_clear(topk_step)
                    for i in (0, 1):
                        dve.tensor_scalar(sel[i], sel[i], MARK, -BIG, ALU.not_equal, ALU.mult
                                          ).then_inc(bias_ready, 1)

            def causal_before(g):
                return sum(1 if selects(i) else 2 for i in range(g))

            def attend(s):
                def logits(g, h):
                    n = HEADS * g + h
                    w, at = width(g), score_at(*divmod(g, R))
                    job = logits_before(g) + h * len(pieces(w))
                    if n >= 2:
                        g2_, h2_ = divmod(n - 2, HEADS)
                        dve.wait_ge(turned, t_attn(g2_, h2_) + len(pieces(width(g2_))))
                    for i, (a, pw) in enumerate(pieces(w)):
                        dve.wait_ge(logit_ready, job + 1)
                        dve.tensor_tensor_reduce(prob[n % 2][:, a:a + pw], bank[job % 4][:, 0:pw],
                                                 scores[:, at + a:at + a + pw], 1.0, NEG, ALU.add, ALU.max,
                                                 accum_out=part_max[:, n % 2, i:i + 1]).then_inc(logit_taken, 1)
                        job += 1
                    dve.wait_ge(logit_taken, job)
                    if n >= 2:
                        dve.wait_ge(exp_done, n - 1)
                    dve.tensor_reduce(neg_max[:, n % 2:n % 2 + 1], part_max[:, n % 2, 0:len(pieces(w))], X_AXIS,
                                      ALU.max, negate=True).then_inc(max_ready, 1)

                def invert_sums(g):
                    dve.wait_ge(exp_done, HEADS * (g + 1))
                    if g % R >= 2:
                        dve.wait_ge(diag_done, g - 1)
                    dve.reciprocal(inv_sum[:, g % 2, :], row_sum[:, g % 2, :]).then_inc(inv_done, 1)

                def normalise(g):
                    r = g % R
                    dve.wait_ge(pv_done, HEADS * (g + 1))
                    dve.wait_ge(turned_taken, t_out(g) + 1)
                    if r >= 2:
                        dve.wait_ge(mix_low, 8 * s + 4 + r - 1)
                    dve.tensor_tensor(o_turned[g % 2], bank[4 + g % 2][:, :], o_scale[g % 2], ALU.mult
                                      ).then_inc(o_normed, 1)

                dve.wait_ge(causal_done, causal_before(row_tile(s, R)))
                dve.wait_ge(bias_ready, R * s + R - TOPK // P)
                if s:
                    dve.wait_ge(act_done, NF * s)
                for r in range(R):
                    g = row_tile(s, r)
                    logits(g, 0)
                    if r:
                        invert_sums(g - 1)
                    for h in range(1, HEADS):
                        logits(g, h)
                        if r and h == 2:
                            normalise(g - 1)
                invert_sums(row_tile(s, R - 1))
                normalise(row_tile(s, R - 1))
                if s + 1 < NSB:
                    norm(("emb", s + 1), lambda half, r: dve.wait_ge(x_loaded[r], 16 * (s + 2)), next_rows)
                norm(("one", s), lambda half, r: dve.wait_ge(mixed_taken, 2 * R * s + R * half + r + 1))

            def feed_forward(s):
                norm(("two", s), lambda half, r: dve.wait_ge(
                    down_added, DOWN_JOBS * (s + 1) - 2 * R + R * half + r + 1))

            def reduce_angle(sin_arg, cos_arg, angle, tmp):
                c1, c2, c3 = split_two_pi()
                link(dve.tensor_scalar(tmp, angle, 1 / TWO_PI, MAGIC, ALU.mult, ALU.add))
                link(dve.tensor_scalar(tmp, tmp, MAGIC, None, ALU.subtract))
                for part in (c1, c2, c3):
                    link(dve.scalar_tensor_tensor(angle, tmp, -part, angle, ALU.mult, ALU.add))
                link(dve.tensor_scalar(sin_arg, angle, 3.1415925, -3.1415925, ALU.min, ALU.max))
                link(dve.tensor_scalar(tmp, sin_arg, -1.0, None, ALU.mult))
                link(dve.tensor_tensor(tmp, tmp, sin_arg, ALU.max))
                link(dve.tensor_scalar(cos_arg, tmp, -1.0, math.pi / 2, ALU.mult, ALU.add))

            def k_(i):
                return s5c[:, i, :]

            norm(("emb", 0), lambda half, r: dve.wait_ge(x_loaded[r], 16))
            lr, li, step, mag = k_(0), k_(1), k_(3), k_(5)
            dve.wait_ge(const_loaded, 16 * CONSTS)
            dve.wait_ge(act_setup, 1)
            link(dve.tensor_tensor(k_(4), lr, step, ALU.mult))
            link(dve.tensor_tensor(k_(10), li, step, ALU.mult))
            link(dve.tensor_copy(pos_f[:, :], pos_i[:, :]))
            reduce_angle(k_(6), k_(7), k_(10), k_(11))
            ang = tmp_c[:, 0:512]
            dve.wait_ge(pool_setup, 3)
            link(dve.tensor_tensor(ang.rearrange("p (g f) -> p g f", g=16),
                                   pos_f[:, :].unsqueeze(2).to_broadcast([P, 16, 32]),
                                   inv_f[:, :].unsqueeze(1).to_broadcast([P, 16, 32]), ALU.mult))
            reduce_angle(tmp_a[:, 0:512], tmp_b[:, 0:512], ang, tmp_d[:, 0:512])
            assert setup_n[0] == SETUP_ANGLES
            dve.wait_ge(act_setup, 3)
            y, z, z2, acc = rgc[:, 8, :], rgc[:, 9, :], rgc[:, 10, :], rgc[:, 11, :]
            link(dve.tensor_scalar(z, y, 2.0, None, ALU.add))
            link(dve.reciprocal(z, z))
            link(dve.tensor_tensor(z, z, y, ALU.mult))
            link(dve.tensor_tensor(z2, z, z, ALU.mult))
            link(dve.tensor_scalar(acc, z2, 1 / 17, 1 / 15, ALU.mult, ALU.add))
            for n in (13, 11, 9, 7, 5, 3, 1):
                link(dve.tensor_tensor(acc, acc, z2, ALU.mult))
                link(dve.tensor_scalar(acc, acc, 1 / n, None, ALU.add))
            link(dve.tensor_tensor(acc, acc, z, ALU.mult))
            link(dve.tensor_scalar(z, rgc[:, 3, :], -1.0, 0.0, ALU.mult, ALU.max))
            link(dve.scalar_tensor_tensor(acc, acc, 2.0, z, ALU.mult, ALU.add))
            link(dve.tensor_scalar(rgc[:, 4, :], acc, -4.0, None, ALU.mult))
            link(dve.tensor_scalar(rgc[:, 5, :], rgc[:, 1, :], 0.5, None, ALU.mult))
            link(dve.tensor_scalar(rgc[:, 6, :], rgc[:, 2, :], 0.5, None, ALU.mult))
            link(dve.tensor_scalar(s5c[:, 20:22, 0], bglu_col[:, :], 0.5, None, ALU.mult))
            dve.wait_ge(act_setup, 5)
            ar, ai, nr, den, cr, ci, t1, t2 = (k_(i) for i in (12, 13, 14, 15, 16, 17, 18, 19))
            link(dve.tensor_tensor(ar, mag, k_(9), ALU.mult))
            link(dve.tensor_tensor(ai, mag, k_(8), ALU.mult))
            link(dve.tensor_tensor(den, lr, lr, ALU.mult))
            link(dve.tensor_tensor(t1, li, li, ALU.mult))
            link(dve.tensor_tensor(den, den, t1, ALU.add))
            link(dve.reciprocal(den, den))
            link(dve.tensor_scalar(nr, ar, -1.0, None, ALU.add))
            link(dve.tensor_tensor(t1, nr, lr, ALU.mult))
            link(dve.tensor_tensor(t2, ai, li, ALU.mult))
            link(dve.tensor_tensor(t1, t1, t2, ALU.add))
            link(dve.tensor_tensor(cr, t1, den, ALU.mult))
            link(dve.tensor_tensor(t1, ai, lr, ALU.mult))
            link(dve.tensor_tensor(t2, nr, li, ALU.mult))
            link(dve.tensor_tensor(t1, t1, t2, ALU.subtract))
            link(dve.tensor_tensor(ci, t1, den, ALU.mult))
            dve.wait_ge(blocks_loaded, 16 * BLOCKS)
            b4 = [t.rearrange("p (i c) -> p i c", c=32) for t in blk_b]
            crb = cr.unsqueeze(2).to_broadcast([P, NST, 32])
            cib = ci.unsqueeze(2).to_broadcast([P, NST, 32])
            s4 = setup[:, 1536:1792].rearrange("p (i c) -> p i c", c=32)
            link(dve.tensor_tensor(b4[2], b4[0], crb, ALU.mult))
            link(dve.tensor_tensor(s4, b4[1], cib, ALU.mult))
            link(dve.tensor_tensor(b4[2], b4[2], s4, ALU.subtract))
            link(dve.tensor_tensor(b4[3], b4[1], crb, ALU.mult))
            link(dve.tensor_tensor(s4, b4[0], cib, ALU.mult))
            link(dve.tensor_tensor(b4[3], b4[3], s4, ALU.add))
            assert setup_n[0] == SETUP_MATRICES
            link(dve.tensor_copy(phase[:, :, 0, 0], k_(9)))
            link(dve.tensor_copy(phase[:, :, 1, 0], k_(8)))
            m = 1
            while m < TW:
                a = ph_a[:, 0:NST * m].rearrange("p (i t) -> p i t", i=NST)
                b = ph_b[:, 0:NST * m].rearrange("p (i t) -> p i t", i=NST)
                lo = [phase[:, :, c, 0:m] for c in (0, 1)]
                by = [phase[:, :, c, m - 1:m].to_broadcast([P, NST, m]) for c in (0, 1)]
                link(dve.tensor_tensor(a, lo[0], by[0], ALU.mult))
                link(dve.tensor_tensor(b, lo[1], by[1], ALU.mult))
                link(dve.tensor_tensor(phase[:, :, 0, m:2 * m], a, b, ALU.subtract))
                link(dve.tensor_tensor(a, lo[0], by[1], ALU.mult))
                link(dve.tensor_tensor(b, lo[1], by[0], ALU.mult))
                link(dve.tensor_tensor(phase[:, :, 1, m:2 * m], a, b, ALU.add))
                m *= 2
            assert setup_n[0] == SETUP_PHASES

            mix_in(0)
            attend(0)
            for s in range(NSB):
                if s + 1 < NSB:
                    mix_in(s + 1)
                feed_forward(s)
                if s + 1 < NSB:
                    attend(s + 1)

        @block.tensor
        def _(pe):
            def arrived(n, k, w):
                if IS_SPLIT[n]:
                    m = SPLIT_OF[n]
                    pe.wait_ge(split_low, m + 1)
                    return [pairs[:, m % SLOTS, i, 0:k * w].rearrange("p (k n) -> p k n", k=k) for i in (0, 1)]
                pe.wait_ge(chunk_loaded[n % SLOTS], 16 * (n // SLOTS + 1))
                return ring[:, n % SLOTS, 0:k * w].rearrange("p (k n) -> p k n", k=k)

            def product(dst, left, right, start, stop):
                first = pe.matmul(dst, left[0], right[0], start=start, stop=False)
                pe.matmul(dst, left[0], right[1], start=False, stop=False)
                return first, pe.matmul(dst, left[1], right[0], start=False, stop=stop)

            def turn(t, blocks):
                if t >= 2:
                    pe.wait_ge(turned_taken, t - 1)
                for i, src in enumerate(blocks):
                    ins = pe.transpose(tbank[t % 2][:, i * P:(i + 1) * P], src, ident[:, :])
                ins.then_inc(turned, 1)

            def turn_queries(t, src):
                turn(t, [src[:, h * HD:h * HD + P] for h in range(4)])
                pe.wait_ge(turned_taken, t)
                dst = tbank[(t + 1) % 2]
                for k in range(3):
                    pe.transpose(dst[:, k * P:(k + 1) * P], src[:, (4 + k) * HD:(4 + k) * HD + P], ident[:, :])
                for m, h in ((0, 7), (1, 0)):
                    ins = pe.matmul(dst[HD * m:HD * (m + 1), 3 * P:4 * P], src[:, h * HD:(h + 1) * HD], ident[:, :],
                                    start=True, stop=True)
                ins.then_inc(turned, 1)

            def norm_turn(call, tiles):
                pe.wait_ge(normed, R * (NORM[call] + 1))
                for k in range(KT):
                    turn(T_AT[call] + k, [tiles[:, r, k * P:(k + 1) * P] for r in range(R)])

            def s5_in(n):
                i = n % NST
                c, j = divmod(i, 4)
                sub = (n % STEPS) // NST
                if n:
                    pe.wait_ge(s5_mixed, 2 * n)
                rhs = u_t[32 * j:32 * j + 32, c, sub * TW:(sub + 1) * TW]
                for m in (0, 1):
                    ins = pe.matmul(bank[4][:, m * TW:(m + 1) * TW], bT[32 * j:32 * j + 32, m, c, :], rhs,
                                    start=True, stop=True)
                ins.then_inc(bu_ready, 1)

            def s5_out(n):
                i = n % NST
                c, j = divmod(i, 4)
                q = n // NST
                pe.wait_ge(s5_state, 2 * n + 1)
                if i == 0 and q:
                    pe.wait_ge(y_taken, 2 * q)
                for m in (0, 1):
                    ins = pe.matmul(bank[5][32 * j:32 * j + 32, c * TW:(c + 1) * TW], cT[:, m, i, :],
                                    s5_x[n % 2][:, m, :], start=(m == 0), stop=(m == 1))
                ins.then_inc(y_ready, 1)

            def features(s):
                norm_turn(("emb", s), next_rows if s else rows)
                t0 = T_AT["emb", s]
                c0 = CHUNK_AT["mix", s]
                for m in range(6):
                    n = 10 * s + m
                    w = arrived(c0 + m, KT, P)
                    if m == 0 and s:
                        pe.wait_ge(o_normed, R * s)
                    if m >= 2:
                        pe.wait_ge(feat_taken, n - 1)
                    for k in range(KT):
                        if m == 0:
                            pe.wait_ge(turned_taken, t0 + k + 1)
                        ins = pe.matmul(bank[4 + n % 2][:, :], w[:, k, :], hT[:, k, :],
                                        start=(k == 0), stop=(k == KT - 1))
                        if k == 0:
                            ins.then_inc(chunk_used, 1)
                    ins.then_inc(feat_ready, 1)

            def mix_in(s):
                t0 = T_AT["mix", s]
                c0 = CHUNK_AT["mix", s]
                pe.wait_ge(conv_done, 8 * (s + 1))
                for m in range(4):
                    n = 10 * s + 6 + m
                    kind, c = divmod(m, 2)
                    pe.wait_ge(feat_taken, n - 1)
                    pe.matmul(bank[4 + n % 2][:, :], w_gates[:, kind, c, :], conv_t[:, c, :], start=True,
                              stop=True).then_inc(feat_ready, 1)
                pe.wait_ge(feat_taken, 10 * (s + 1))
                for t, slot in enumerate(SLOT_LIST):
                    kind, part, r = slot
                    if kind in GROUP_OF:
                        job = 3 * R * s + R * GROUP_OF[kind] + r
                        if part == 0:
                            if kind != "q":
                                pe.wait_ge(proj_taken, job - 3)
                            elif s and r == 0:
                                pe.wait_ge(mixed_taken, 2 * R * s)
                        c = c0 + 6 + {"q": 0, "kv": 4, "qi": 6}[kind] + part
                        nk, wide = (4, 256) if kind == "kv" else (2, 512)
                        w = arrived(c, nk, wide)
                        for i in range(nk):
                            k = nk * part + i
                            ins = pe.matmul(bank[r][:, 0:wide], hT[:, k, r * P:(r + 1) * P], w[:, i, :],
                                            start=(k == 0), stop=(k == KT - 1))
                            if r == 0 and i == 0:
                                ins.then_inc(chunk_used, 1)
                        if part == GROUP_CHUNKS[kind] - 1:
                            if kind == "kv":
                                for k in range(KT):
                                    ins = pe.matmul(bank[r][:, 256:256 + N_IN - C_KI], hT[:, k, r * P:(r + 1) * P],
                                                    w_tail[:, k, :], start=(k == 0), stop=(k == KT - 1))
                            ins.then_inc(proj_ready, 1)
                    n = s5_step_of(t)
                    if n is not None and n < STEPS:
                        s5_in(STEPS * s + n)
                    if n is not None and n >= 2:
                        s5_out(STEPS * s + n - 2)
                    j = transposed_in(slot)
                    if j is not None:
                        pe.wait_ge(rope_done, 3 * R * s + j + 1)
                        src = roped[j % R]
                        if j < 2 * R:
                            turn(t0 + j, [src[:, i * P:(i + 1) * P] for i in range(4 if j < R else 2)])
                        else:
                            turn_queries(t0 + turned_banks(j)[0], src)
                pe.wait_ge(gl_dve, 2 * s + 1)
                pe.wait_ge(y_taken, 4 * (s + 1))
                for c in (0, 1):
                    for k in (0, 1):
                        ins = pe.matmul(bank[4 + c][:, :], w_glu[:, k, c * P:(c + 1) * P], u_t[:, k, :],
                                        start=(k == 0), stop=(k == 1))
                    ins.then_inc(glu_ready, 1)
                pe.wait_ge(proj_taken, 3 * R * (s + 1))
                pe.wait_ge(turned_taken, t0 + 4 * R)
                n = idx_before(s)
                for r, h, a, w in idx_jobs(s):
                    if n >= 4:
                        pe.wait_ge(idx_taken, n - 3)
                    for m in (0, 1):
                        ins = pe.matmul(bank[n % 4][:, 0:w], idx_qT[:, h, r * P:(r + 1) * P],
                                        idx_keys[:, m, a:a + w], start=(m == 0), stop=(m == 1))
                    ins.then_inc(idx_ready, 1)
                    n += 1

            def attend(s):
                def logits(g, h):
                    q = 64 * (h // 4)
                    r = g % R
                    job = logits_before(g) + h * len(pieces(width(g)))
                    for a, w in pieces(width(g)):
                        if job >= 4:
                            pe.wait_ge(logit_taken, job - 3)
                        pe.matmul(bank[job % 4][:, 0:w], qT[q:q + 64, h % 4, r * P:(r + 1) * P],
                                  keysT[q:q + 64, a:a + w], start=True, stop=True).then_inc(logit_ready, 1)
                        job += 1

                def values(g, h):
                    n = HEADS * g + h
                    t = t_attn(g, h)
                    kv = h // 4
                    parts = pieces(width(g))
                    pe.wait_ge(exp_done, n + 1)
                    if h == 0 and g >= 2:
                        pe.wait_ge(o_normed, g - 1)

                    def turn_part(i):
                        a, w = parts[i]
                        turn(t + i, [prob[n % 2][:, a + b:a + b + P] for b in range(0, w, P)])

                    turn_part(0)
                    for i, (a, w) in enumerate(parts):
                        if i + 1 < len(parts):
                            turn_part(i + 1)
                        pe.wait_ge(turned_taken, t + i + 1)
                        for b in range(0, w, P):
                            kt = (a + b) // P
                            ins = pe.matmul(
                                bank[4 + g % 2][HD * (h % 2):HD * (h % 2 + 1), (h // 2) * P:(h // 2 + 1) * P],
                                vals[:, kt, kv * HD:(kv + 1) * HD], probT[n % 2][:, a + b:a + b + P],
                                start=(kt == 0), stop=(kt == g))
                    ins.then_inc(pv_done, 1)

                def spread_scales(g):
                    t = t_out(g)
                    pe.wait_ge(diag_done, g + 1)
                    pe.wait_ge(turned_taken, t - 1)
                    for m in (0, 1):
                        ins = pe.matmul(tbank[t % 2][HD * m:HD * (m + 1), :], ones[:, :], inv_diag[:, m::2, :],
                                        start=True, stop=True)
                    ins.then_inc(turned, 1)

                pe.wait_ge(idx_taken, idx_before(s + 1))
                if s:
                    pe.wait_ge(down_taken, DOWN_JOBS * s)
                    pe.wait_ge(up_taken, 3 * NF * s)
                else:
                    pe.wait_ge(proj_taken, 3 * R)
                    pe.wait_ge(glu_taken, 2)
                order = [(row_tile(s, r), h) for r in range(R) for h in range(HEADS)]
                logits(*order[0])
                for i, (g, h) in enumerate(order):
                    if i + 1 < len(order):
                        logits(*order[i + 1])
                    values(g, h)
                    if h == 0 and g % R:
                        spread_scales(g - 1)
                spread_scales(row_tile(s, R - 1))
                c0 = CHUNK_AT["att", s]
                pe.wait_ge(logit_taken, logits_before(row_tile(s, R)))
                for c in (0, 1):
                    for q in range(4):
                        if c == 0:
                            pe.wait_ge(mix_low, 8 * s + (4 if q < 2 else 8))
                        w = arrived(c0, 2, 512)
                        for r in range(R):
                            if c and q == 0:
                                pe.wait_ge(mixed_taken, 2 * R * s + r + 1)
                            for i in (0, 1):
                                k = 2 * q + i
                                first, _ = product(bank[r][:, :], [m[k][:, r * P:(r + 1) * P] for m in mix_pair],
                                                   [m[:, i, :] for m in w], start=(k == 0), stop=False)
                                if r == 0 and i == 0:
                                    first.then_inc(chunk_used, 1)
                        c0 += 1
                    for q in (0, 1):
                        w = arrived(c0, 2, 512)
                        for r in range(R):
                            for i in (0, 1):
                                k = 2 * q + i
                                ins = pe.matmul(bank[r][:, k * P:(k + 1) * P], w[:, i, r * P:(r + 1) * P],
                                                alpha_i[:, :], start=False, stop=(k == 3))
                                if r == 0 and i == 0:
                                    ins.then_inc(chunk_used, 1)
                            if q:
                                ins.then_inc(mixed_ready, 1)
                        c0 += 1

            def feed_forward(s):
                pe.wait_ge(p_loaded, 16 * (s + 1))
                for k in range(D_PLE // P):
                    turn(T_AT["ffn", s] + k, [p_rows[:, r, k * P:(k + 1) * P] for r in range(R)])
                pe.wait_ge(turned_taken, T_AT["ffn", s] + D_PLE // P)
                c0 = CHUNK_AT["ffn", s]
                if s + 1 < NSB:
                    pe.wait_ge(glu_taken, 2 * (s + 2))
                    pe.wait_ge(idx_taken, idx_before(s + 2))
                else:
                    pe.wait_ge(o_normed, R * (s + 1))
                    pe.wait_ge(mixed_taken, 2 * R * (s + 1))
                for c in (0, 1):
                    w = arrived(c0, 2, 512)
                    for r in range(R):
                        n = 2 * R * s + R * c + r
                        if n % (2 * R) >= 2:
                            pe.wait_ge(pp_taken, n - 1)
                        for k in (0, 1):
                            ins = pe.matmul(bank[4 + n % 2][:, :], pT[:, k, r * P:(r + 1) * P], w[:, k, :],
                                            start=(k == 0), stop=(k == 1))
                            if r == 0 and k == 0:
                                ins.then_inc(chunk_used, 1)
                        ins.then_inc(pp_ready, 1)
                    c0 += 1
                    for q in range(4):
                        w = arrived(c0, 2, 512)
                        for r in range(R):
                            n = 2 * R * s + R * c + r
                            if c and q == 0:
                                pe.wait_ge(pg_taken, n - R + 1)
                            for i in (0, 1):
                                k = 2 * q + i
                                if c == 0 and r == 0:
                                    pe.wait_ge(h1_split, 2 * KT * s + KT + k + 1)
                                first, ins = product(bank[r][:, :], [m[:, k, r * P:(r + 1) * P] for m in h1_pair],
                                                     [m[:, i, :] for m in w], start=(k == 0), stop=(k == KT - 1))
                                if r == 0 and i == 0:
                                    first.then_inc(chunk_used, 1)
                            if q == 3:
                                ins.then_inc(pg_ready, 1)
                        c0 += 1
                pe.wait_ge(pp_taken, 2 * R * (s + 1))
                for kind, i in FFN_STEPS:
                    if kind == "up":
                        f = NF * s + i
                        if i >= 2:
                            pe.wait_ge(up_taken, 3 * (f - 1))
                        for m in (0, 1):
                            w = arrived(c0, KT, P)
                            for k in range(KT):
                                first, ins = product(bank[4 + 2 * (f % 2) + m][:, :], [t[:, k, :] for t in w],
                                                     [t[:, k, :] for t in h1_pair], start=(k == 0), stop=(k == KT - 1))
                                if k == 0:
                                    first.then_inc(chunk_used, 1)
                            ins.then_inc(up_ready, 1)
                            c0 += 1
                        continue
                    f0, count = PARTS[i]
                    for c in (0, 1):
                        for a in range(0, count, 2):
                            w = arrived(c0, 2, 512)
                            for r in range(R):
                                n = DOWN_JOBS * s + 2 * R * i + R * c + r
                                if a == 0:
                                    if i == 0 and c == 0:
                                        pe.wait_ge(pg_taken, 2 * R * (s + 1))
                                    else:
                                        pe.wait_ge(down_taken, n - R + 1)
                                for k in (a, a + 1):
                                    if r == 0 and c == 0:
                                        pe.wait_ge(act_done, NF * s + f0 + k + 1)
                                    last = k == count - 1 and i < len(PARTS) - 1
                                    first, ins = product(
                                        bank[r][:, :], [t[(f0 + k) % ACTS][:, r * P:(r + 1) * P] for t in act_pair],
                                        [t[:, k - a, :] for t in w], start=(k == 0), stop=last)
                                    if r == 0 and k == a:
                                        first.then_inc(chunk_used, 1)
                                if last:
                                    ins.then_inc(down_ready, 1)
                                if k == count - 1 and i == len(PARTS) - 1:
                                    for k in range(4):
                                        for m in (0, 1):
                                            ins = pe.matmul(bank[r][:, k * P:(k + 1) * P],
                                                            h1_pair[m][:, 4 * c + k, r * P:(r + 1) * P].bitcast(f32),
                                                            alpha_i[:, :], start=False, stop=(k == 3 and m == 1))
                                    ins.then_inc(down_ready, 1)
                            c0 += 1

            pe.wait_ge(pool_setup, 3)
            features(0)
            t = T_AT["setup", 0]
            pe.wait_ge(dve_setup, SETUP_MATRICES)
            turn(t, [blk_b[2 + m][:, c * P:(c + 1) * P] for m in (0, 1) for c in (0, 1)])
            turn(t + 1, [blk_c[m][:, c * P:(c + 1) * P] for m in (0, 1) for c in (0, 1)])
            pe.wait_ge(turned_taken, t + 2)

            mix_in(0)
            attend(0)
            for s in range(NSB):
                if s + 1 < NSB:
                    features(s + 1)
                norm_turn(("one", s), rows)
                if s + 1 < NSB:
                    mix_in(s + 1)
                feed_forward(s)
                if s + 1 < NSB:
                    attend(s + 1)


_INS = ["x", "p", "positions", "ln_emb_g", "ln_emb_b", "w_in",
        "s5_lam_re", "s5_lam_im", "s5_log_step", "s5_b_re", "s5_b_im", "s5_c_re", "s5_c_im",
        "s5_d", "s5_w_glu", "s5_b_glu",
        "rg_conv_w", "rg_conv_b", "rg_wa", "rg_ba", "rg_wx", "rg_bx", "rg_lam",
        "w_out", "ln1_g", "ln1_b", "ffn_w_up", "ffn_w_down", "ple_w_gate", "ple_w_proj",
        "ln2_g", "ln2_b"]


def kernel(**inputs):
    import concourse.bacc as bacc
    from concourse.bass_utils import run_bass_kernel_spmd

    nc = bacc.Bacc("TRN2", target_bir_lowering=False, num_devices=1, dynamic_dma_scratch_size=1024)
    arrays, args = {}, []
    for name in _INS:
        a = np.ascontiguousarray(inputs[name])
        arrays[f"in_{name}_dram"] = a
        args.append(nc.dram_tensor(f"in_{name}_dram", a.shape, mybir.dt.from_np(a.dtype), kind="ExternalInput").ap())
    out = nc.dram_tensor("out_0_dram", (1, SEQ, D), mybir.dt.float32, kind="ExternalOutput").ap()
    h_spill = nc.dram_tensor("h_spill", (NSB, P, KT, SB), mybir.dt.float32, kind="Internal").ap()
    phase_spill = nc.dram_tensor("phase_spill", (P, NST, 2, TW), mybir.dt.float32, kind="Internal").ap()
    trunk_kernel(nc, *args, out, h_spill, phase_spill)
    r = run_bass_kernel_spmd(nc, [arrays], core_ids=[0])
    return r.results[0]["out_0_dram"]
```
